# Optimizing a Trainium2 kernel written in Bass

```python
import math
import jax, jax.numpy as jnp
from jax import lax
import numpy as np

D_MODEL = 1024
BATCH = 1
SEQ = 2048
DEPTH = 1

CHUNK = 64
HEAD_DIM = 64
ROPE_THETA = 10000.0
NORM_EPS = 1e-6
NEG_INF = -1e30
A_Q_HEADS = 8
A_KV_HEADS = 2
A_GROUP = A_Q_HEADS // A_KV_HEADS
WINDOW = 128
A_BAND = WINDOW // CHUNK
B_HEADS = 8
B_PREV_CHUNKS = 8
B_BAND = B_PREV_CHUNKS + 1
REL_CLIP = 256
N_REL = 2 * REL_CLIP + 1
A_Q_W = A_Q_HEADS * HEAD_DIM
A_KV_W = A_KV_HEADS * HEAD_DIM
B_W = B_HEADS * HEAD_DIM
MIX_W = A_Q_W + B_W
D_IN = A_Q_W + 2 * A_KV_W + 3 * B_W
MEM_LEN = 256
X_HEADS = 4
X_HEAD_DIM = D_MODEL // X_HEADS
D_FF = -(-8 * D_MODEL // (3 * 256)) * 256

kernel_name = 'hymba_style_chunk_streaming_block'

def rmsnorm(x, g):
    xf = x.astype(jnp.float32)
    y = xf * lax.rsqrt(jnp.mean(xf * xf, axis=-1, keepdims=True) + NORM_EPS)
    return (y * g.astype(jnp.float32)).astype(x.dtype)

def rotary(t, positions):
    half = HEAD_DIM // 2
    inv_freq = 1.0 / (ROPE_THETA ** (jnp.arange(half, dtype=jnp.float32) * (2.0 / HEAD_DIM)))
    ang = positions.astype(jnp.float32)[..., None] * inv_freq
    cos = jnp.cos(ang)[:, :, None, :]
    sin = jnp.sin(ang)[:, :, None, :]
    tf = t.astype(jnp.float32)
    t1, t2 = tf[..., :half], tf[..., half:]
    return jnp.concatenate([t1 * cos - t2 * sin, t2 * cos + t1 * sin], axis=-1).astype(t.dtype)

def chunk_band(t, n_band):
    b, s, h, d = t.shape
    nc = s // CHUNK
    tc = t.reshape(b, nc, CHUNK, h, d)
    tp = jnp.pad(tc, ((0, 0), (n_band - 1, 0), (0, 0), (0, 0), (0, 0)))
    idx = jnp.arange(nc)[:, None] + jnp.arange(n_band)[None, :]
    return tp[:, idx].reshape(b, nc, n_band * CHUNK, h, d)

def band_valid(nc, n_band):
    cidx = jnp.arange(nc)[:, None] - (n_band - 1) + jnp.arange(n_band)[None, :]
    return jnp.repeat(cidx >= 0, CHUNK, axis=1)

def window_sink_gqa(q, k, v, sinks):
    b, s = q.shape[:2]
    nc = s // CHUNK
    qc = q.reshape(b, nc, CHUNK, A_KV_HEADS, A_GROUP, HEAD_DIM)
    kb = chunk_band(k, A_BAND)
    vb = chunk_band(v, A_BAND)
    sc = jnp.einsum('bncvgd,bnlvd->bnvgcl', qc, kb).astype(jnp.float32) * (HEAD_DIM ** -0.5)
    valid = band_valid(nc, A_BAND)[None, :, None, None, None, :]
    sc = jnp.where(valid, sc, NEG_INF)
    sink = sinks.astype(jnp.float32).reshape(1, 1, A_KV_HEADS, A_GROUP, 1, 1)
    m = jnp.maximum(jnp.max(sc, axis=-1, keepdims=True), sink)
    p = jnp.exp(sc - m)
    p = p / (jnp.sum(p, axis=-1, keepdims=True) + jnp.exp(sink - m))
    o = jnp.einsum('bnvgcl,bnlvd->bncvgd', p.astype(v.dtype), vb)
    return o.reshape(b, s, A_Q_W)

def chunk_relbias_attention(q, k, v, rel_bias):
    b, s = q.shape[:2]
    nc = s // CHUNK
    band_len = B_BAND * CHUNK
    qc = q.reshape(b, nc, CHUNK, B_HEADS, HEAD_DIM)
    kb = chunk_band(k, B_BAND)
    vb = chunk_band(v, B_BAND)
    rel = (B_BAND - 1) * CHUNK + jnp.arange(CHUNK)[:, None] - jnp.arange(band_len)[None, :]
    rel = jnp.clip(rel, -REL_CLIP, REL_CLIP) + REL_CLIP
    bias = rel_bias.astype(jnp.float32)[:, rel]
    sc = jnp.einsum('bnchd,bnlhd->bnhcl', qc, kb).astype(jnp.float32) * (HEAD_DIM ** -0.5) + bias
    valid = band_valid(nc, B_BAND)[None, :, None, None, :]
    sc = jnp.where(valid, sc, NEG_INF)
    p = jax.nn.softmax(sc, axis=-1)
    o = jnp.einsum('bnhcl,bnlhd->bnchd', p.astype(v.dtype), vb)
    return o.reshape(b, s, B_W)

def memory_cross_attention(h, mem_n, w_cq, w_ckv, w_co):
    b, s, _ = h.shape
    q = (h @ w_cq).reshape(b, s, X_HEADS, X_HEAD_DIM)
    kv = mem_n @ w_ckv
    k = kv[..., :D_MODEL].reshape(b, -1, X_HEADS, X_HEAD_DIM)
    v = kv[..., D_MODEL:].reshape(b, -1, X_HEADS, X_HEAD_DIM)
    sc = jnp.einsum('bshd,bmhd->bhsm', q, k).astype(jnp.float32) * (X_HEAD_DIM ** -0.5)
    p = jax.nn.softmax(sc, axis=-1)
    o = jnp.einsum('bhsm,bmhd->bshd', p.astype(v.dtype), v).reshape(b, s, D_MODEL)
    return o @ w_co

def setup_inputs(seed: int = 0) -> dict:
    key = jax.random.key(seed)
    ks = jax.random.split(key, 24)
    f32 = jnp.float32

    def nrm(k, shape, scale):
        return jax.random.normal(k, shape, f32) * scale

    def gain(k, n):
        return 1.0 + 0.05 * jax.random.normal(k, (DEPTH, n), f32)

    x = jax.random.normal(ks[0], (BATCH, SEQ, D_MODEL), f32)
    mem = jax.random.normal(ks[1], (BATCH, MEM_LEN, D_MODEL), f32)
    offset = jax.random.randint(ks[2], (BATCH, 1), 0, 4096, dtype=jnp.int32)
    positions = (offset + jnp.arange(SEQ, dtype=jnp.int32)[None, :]).astype(jnp.int32)
    return {
        'x': x,
        'mem': mem,
        'positions': positions,
        'g_mix': gain(ks[3], D_MODEL),
        'w_in': nrm(ks[4], (DEPTH, D_MODEL, D_IN), D_MODEL ** -0.5),
        'b_in': nrm(ks[5], (DEPTH, D_IN), 0.02),
        'sinks': nrm(ks[6], (DEPTH, A_Q_HEADS), 0.5),
        'rel_bias': nrm(ks[7], (DEPTH, B_HEADS, N_REL), 0.1),
        'g_grp_a': gain(ks[8], A_Q_W),
        'g_grp_b': gain(ks[9], B_W),
        'w_out': nrm(ks[10], (DEPTH, MIX_W, D_MODEL), MIX_W ** -0.5),
        'g_cross': gain(ks[11], D_MODEL),
        'g_mem': gain(ks[12], D_MODEL),
        'w_cq': nrm(ks[13], (DEPTH, D_MODEL, D_MODEL), D_MODEL ** -0.5),
        'w_ckv': nrm(ks[14], (DEPTH, D_MODEL, 2 * D_MODEL), D_MODEL ** -0.5),
        'w_co': nrm(ks[15], (DEPTH, D_MODEL, D_MODEL), D_MODEL ** -0.5),
        'g_ffn': gain(ks[16], D_MODEL),
        'w_gate': nrm(ks[17], (DEPTH, D_MODEL, D_FF), D_MODEL ** -0.5),
        'w_up': nrm(ks[18], (DEPTH, D_MODEL, D_FF), D_MODEL ** -0.5),
        'w_down': nrm(ks[19], (DEPTH, D_FF, D_MODEL), D_FF ** -0.5),
        'g_final': 1.0 + 0.05 * jax.random.normal(ks[20], (D_MODEL,), f32),
    }

def reference(x, mem, positions, g_mix, w_in, b_in, sinks, rel_bias, g_grp_a, g_grp_b, w_out,
              g_cross, g_mem, w_cq, w_ckv, w_co, g_ffn, w_gate, w_up, w_down, g_final):
    b, s, _ = x.shape
    s1 = A_Q_W
    s2 = s1 + A_KV_W
    s3 = s2 + A_KV_W
    s4 = s3 + B_W
    s5 = s4 + B_W
    for l in range(DEPTH):
        h = rmsnorm(x, g_mix[l])
        proj = h @ w_in[l] + b_in[l]
        qa = rotary(proj[..., :s1].reshape(b, s, A_Q_HEADS, HEAD_DIM), positions)
        ka = rotary(proj[..., s1:s2].reshape(b, s, A_KV_HEADS, HEAD_DIM), positions)
        va = proj[..., s2:s3].reshape(b, s, A_KV_HEADS, HEAD_DIM)
        qb = proj[..., s3:s4].reshape(b, s, B_HEADS, HEAD_DIM)
        kb = proj[..., s4:s5].reshape(b, s, B_HEADS, HEAD_DIM)
        vb = proj[..., s5:].reshape(b, s, B_HEADS, HEAD_DIM)
        oa = window_sink_gqa(qa, ka, va, sinks[l])
        ob = chunk_relbias_attention(qb, kb, vb, rel_bias[l])
        mix = jnp.concatenate([rmsnorm(oa, g_grp_a[l]), rmsnorm(ob, g_grp_b[l])], axis=-1)
        x = x + mix @ w_out[l]
        h = rmsnorm(x, g_cross[l])
        x = x + memory_cross_attention(h, rmsnorm(mem, g_mem[l]), w_cq[l], w_ckv[l], w_co[l])
        h = rmsnorm(x, g_ffn[l])
        x = x + (jax.nn.silu(h @ w_gate[l]) * (h @ w_up[l])) @ w_down[l]
    return rmsnorm(x, g_final)


_drawn_inputs = setup_inputs


def setup_inputs(seed=0):
    import zlib

    import numpy as np

    out = dict(_drawn_inputs(seed))
    spreads = {}
    factors = {'sinks': 8.0, 'g_cross': 8.0, 'g_mem': 8.0, 'g_ffn': 8.0}
    for name, (base, spread) in spreads.items():
        noise = np.random.default_rng([zlib.crc32(name.encode()), seed]).standard_normal(out[name].shape)
        drawn = base * np.exp(spread * noise) if base else spread * noise
        out[name] = __import__('jax').numpy.asarray(drawn.astype(out[name].dtype))
    for name, factor in factors.items():
        out[name] = (out[name] * factor).astype(out[name].dtype)
    return out
```

```python
import math
from contextlib import ExitStack, nullcontext

import numpy as np

import concourse.bass as bass
from concourse import mybir

F32 = mybir.dt.float32
F32R = mybir.dt.float32r
I32 = mybir.dt.int32
ALU = mybir.AluOpType
ACT = mybir.ActivationFunctionType
AX = mybir.AxisListType

P = 128
D = 1024
SEQ = 2048
HALF = SEQ // 2
KT = D // P
NT = SEQ // P
HT = HALF // P
BANK = 512
HD = 64
CHUNK = 64
EPS = 1e-6
THETA = 10000.0
NEG = -1e30
A_Q, A_KV, B_W = 512, 128, 512
N_PAIR = 4
A_WIN, B_WIN = 2, 5
REL_CLIP = 256
N_REL = 2 * REL_CLIP + 1
MEM = 256
MT = MEM // P
XH, XD = 4, 256
FF = 2816
FT = FF // P
V_GROUP = 320
N_QK = 14
N_QK_A = 6
EXT = 768


def split3(pe, out, l_hi, l_lo, r_hi, r_lo, first, last):
    pe.matmul(out, l_hi, r_hi, start=first, stop=False)
    pe.matmul(out, l_hi, r_lo, start=False, stop=False)
    return pe.matmul(out, l_lo, r_hi, start=False, stop=last)


def raw(ap):
    return ap.bitcast(F32)


class Room:

    def __init__(self, nc, ctx, stage):
        self.nc, self.ctx, self.stage, self.sems = nc, ctx, stage, []
        ctx.callback(self.close)
        self.s_gate = self.sem("s_gate")

    def gate(self, engine):
        engine.sem_inc(self.s_gate, 1)

    def sb(self, name, shape, dt=F32):
        return self.ctx.enter_context(self.nc.sbuf_tensor(f"{self.stage}_{name}", shape, dt))

    def bank(self, name, n=1):
        return self.ctx.enter_context(self.nc.psum_tensor(f"{self.stage}_{name}", [P, n * BANK], F32))

    def sem(self, name):
        semaphore = self.nc.alloc_semaphore(f"{self.stage}_{name}")
        self.sems.append(semaphore)
        return semaphore

    def close(self):
        self.nc.clear_and_free_semaphores(self.sems)
        self.nc.all_engine_barrier()


RING = 2


def made(n):
    return n + 1 + RING


def free(n):
    return n + 1


class Norm:

    def __init__(self, room, groups=1, x=None):
        self.room = room
        self.groups = groups
        self.x = room.sb("x", [P, 2, D]) if x is None else x
        self.xn = room.sb("xn", [P, 2, D])
        self.gain = room.sb("gain", [P, D])
        self.ss = room.sb("ss", [P, 2, groups])
        self.ms = room.sb("ms", [P, 2, groups])
        self.rs = room.sb("rs", [P, 2, groups])
        self.power = room.sb("power", [P, groups])
        self.turned = [room.bank(f"turned{b}") for b in range(2)]
        self.s_gain = room.sem("s_gain")
        self.s_x = [room.sem(f"s_x{j}") for j in range(2)]
        self.s_ss = room.sem("s_ss")
        self.s_ms = room.sem("s_ms")
        self.s_rs = room.sem("s_rs")
        self.s_xn = room.sem("s_xn")
        self.s_turned = room.sem("s_turned")
        self.s_hi = room.sem("s_turned_hi")
        self.s_lo = room.sem("s_turned_lo")
        self.s_power = room.sem("s_power")

    def start_act(self, act):
        act.sem_inc(self.s_ss, RING)

    def start_pool(self, pool):
        pool.memset(self.power[:, :], -0.5).then_inc(self.s_power, 1)
        pool.sem_inc(self.s_rs, RING)
        pool.wait_ge(self.s_power, 1)

    def start_dve(self, dve):
        dve.sem_inc(self.s_xn, RING)
        dve.sem_inc(self.s_lo, RING)
        dve.wait_ge(self.s_gain, 16)

    def start_pe(self, pe):
        pe.sem_inc(self.s_turned, 2 * RING)

    def act_square(self, act, n, j, use):
        x = self.x[:, j, :]
        if use is not None:
            act.wait_ge(self.s_x[j], 16 * use + 16)
        act.wait_ge(self.s_rs, free(n))
        act.wait_ge(self.s_turned, 2 * n + 2)
        w = D // self.groups
        for g in range(self.groups):
            last = act.activation(self.xn[:, j, g * w:(g + 1) * w], x[:, g * w:(g + 1) * w],
                                  ACT.Square, accum_out=self.ss[:, j, g:g + 1])
        last.then_inc(self.s_ss, 1)

    def pool_rsqrt(self, pool, n, j):
        pool.wait_ge(self.s_ss, made(n))
        pool.wait_ge(self.s_xn, free(n))
        self.room.gate(pool)
        pool.tensor_scalar(self.ms[:, j, :], self.ss[:, j, :], float(self.groups) / D, EPS,
                           ALU.mult, ALU.add).then_inc(self.s_ms, 1)
        pool.wait_ge(self.s_ms, n + 1)
        pool.tensor_tensor(self.rs[:, j, :], self.ms[:, j, :], self.power[:, :],
                           ALU.pow).then_inc(self.s_rs, 1)

    def dve_scale(self, dve, n, j):
        x = self.x[:, j, :]
        dve.wait_ge(self.s_rs, made(n))
        dve.wait_ge(self.s_turned, 2 * n + 2)
        w = D // self.groups
        for g in range(self.groups):
            cols = slice(g * w, (g + 1) * w)
            last = dve.scalar_tensor_tensor(self.xn[:, j, cols], x[:, cols], self.rs[:, j, g:g + 1],
                                            self.gain[:, cols], ALU.mult, ALU.mult)
        last.then_inc(self.s_xn, 1)

    def pe_turn(self, pe, ident, n, j):
        pe.wait_ge(self.s_xn, made(n))
        for b in range(2):
            pe.wait_ge(self.s_lo, 2 * n + b + 1)
            for q in range(4):
                k = 4 * b + q
                last = pe.transpose(self.turned[b][:, q * P:(q + 1) * P],
                                    self.xn[:, j, k * P:(k + 1) * P], ident)
            last.then_inc(self.s_turned, 1)

    def act_hi(self, act, n, b, out):
        act.wait_ge(self.s_turned, 2 * n + b + 1 + 2 * RING)
        act.activation(out, self.turned[b][:, :].rearrange("p (k t) -> p k t", k=4),
                       ACT.Copy).then_inc(self.s_hi, 1)

    def dve_lo(self, dve, n, b, out, hi):
        dve.wait_ge(self.s_hi, 2 * n + b + 1)
        dve.tensor_tensor(out, self.turned[b][:, :].rearrange("p (k t) -> p k t", k=4), raw(hi),
                          ALU.subtract).then_inc(self.s_lo, 1)


def make_identity(room, pool, ident, s_ident):
    pool.memset(ident[:, :], 0.0).then_inc(s_ident, 1)
    pool.wait_ge(s_ident, 1)
    pool.affine_select(out=ident[:, :], in_=ident[:, :], compare_op=ALU.not_equal, fill=1.0, base=0,
                       pattern=[[-1, P]], channel_multiplier=1).then_inc(s_ident, 1)


def stage_tables(nc, positions, freq, rel_rev, cos_d, sin_d, ext_d, bias_d):
    with ExitStack() as ctx:
        room = Room(nc, ctx, "tables")
        pos_i = room.sb("pos_i", [P, SEQ], I32)
        ang = room.sb("ang", [P, SEQ])
        turns = room.sb("turns", [P, SEQ])
        turns_i = room.sb("turns_i", [P, SEQ], I32)
        wrap = room.sb("wrap", [P, SEQ])
        sin = room.sb("sin", [P, SEQ])
        cos = room.sb("cos", [P, SEQ])
        fr = room.sb("fr", [P, 2])
        rel = room.sb("rel", [P, 8, N_REL])
        ext = room.sb("ext", [P, 8, EXT])
        band = room.sb("band", [P, 8, B_WIN * P])
        s_mask = room.sem("s_mask")
        s_in = room.sem("s_in")
        s_rel = room.sem("s_rel")
        s_v = room.sem("s_v")
        s_sin = room.sem("s_sin")
        s_act = room.sem("s_act")
        s_ext = room.sem("s_ext")
        s_out = room.sem("s_out")
        two_pi = 2.0 * math.pi
        c1 = 6.28125
        c2 = float(np.float32(np.round((two_pi - c1) * 2.0 ** 21) / 2.0 ** 21))
        c3 = two_pi - c1 - c2
        pi_in = 3.1415925

        with nc.Block() as block:
            @block.sync
            def _(sp):
                sp.dma_start(pos_i[:, :], positions.to_broadcast([P, SEQ])).then_inc(s_in, 16)
                sp.dma_start(fr[:, :], freq).then_inc(s_in, 16)
                sp.dma_start(rel[:, :, :].rearrange("p h r -> p (h r)"),
                             rel_rev.rearrange("(a h) r -> a (h r)", a=1).to_broadcast([P, 8 * N_REL])
                             ).then_inc(s_rel, 16)
                sp.wait_ge(s_sin, 1)
                sp.dma_start(sin_d, sin[:, :]).then_inc(s_out, 16)
                sp.wait_ge(s_act, 2)
                sp.dma_start(cos_d, cos[:, :]).then_inc(s_out, 16)
                sp.wait_ge(s_ext, 2)
                sp.dma_start(ext_d, ext[:, :, :].rearrange("p h n -> p (h n)")).then_inc(s_out, 16)
                sp.wait_ge(s_out, 48)
                win = B_WIN * P
                rows = bass.AP(ext_d.tensor, P - 1, [[8 * EXT - 1, P], [EXT, 8], [1, win]])
                sp.dma_start(band[:, :, :], rows).then_inc(s_in, 16)
                sp.wait_ge(s_mask, 2)
                sp.dma_start(bias_d.rearrange("h p n -> p h n"), band[:, :, :]).then_inc(s_out, 16)
                sp.wait_ge(s_out, 64)

            @block.vector
            def _(dve):
                done = [0]

                def then(instruction):
                    done[0] += 1
                    instruction.then_inc(s_v, 1)
                    dve.wait_ge(s_v, done[0])

                dve.wait_ge(s_in, 32)
                then(dve.tensor_copy(ang[:, :], pos_i[:, :]))
                then(dve.tensor_scalar(ang[:, :], ang[:, :], fr[:, 0:1], None, ALU.mult))
                then(dve.tensor_scalar(turns[:, :], ang[:, :], 1.0 / two_pi, None, ALU.mult))
                then(dve.tensor_copy(turns_i[:, :], turns[:, :]))
                then(dve.tensor_copy(turns[:, :], turns_i[:, :]))
                for c in (c1, c2, c3):
                    then(dve.scalar_tensor_tensor(ang[:, :], turns[:, :], -c, ang[:, :], ALU.mult, ALU.add))
                for _ in range(1):
                    then(dve.tensor_scalar(wrap[:, :], ang[:, :], math.pi, -two_pi, ALU.is_gt, ALU.mult))
                    then(dve.tensor_tensor(ang[:, :], ang[:, :], wrap[:, :], ALU.add))
                    then(dve.tensor_scalar(wrap[:, :], ang[:, :], -math.pi, two_pi, ALU.is_lt, ALU.mult))
                    then(dve.tensor_tensor(ang[:, :], ang[:, :], wrap[:, :], ALU.add))
                then(dve.tensor_scalar(turns[:, :], ang[:, :], math.pi / 2, None, ALU.add))
                then(dve.tensor_scalar(wrap[:, :], turns[:, :], math.pi, -two_pi, ALU.is_gt, ALU.mult))
                then(dve.tensor_tensor(turns[:, :], turns[:, :], wrap[:, :], ALU.add))
                then(dve.tensor_scalar(turns[:, :], turns[:, :], pi_in, -pi_in, ALU.min, ALU.max))
                then(dve.tensor_scalar(ang[:, :], ang[:, :], pi_in, -pi_in, ALU.min, ALU.max))
                dve.wait_ge(s_act, 1)
                dve.tensor_scalar(sin[:, :], sin[:, :], fr[:, 1:2], None, ALU.mult).then_inc(s_sin, 1)

            @block.gpsimd
            def _(pool):
                flat = (B_WIN * P - 1) - REL_CLIP
                pool.wait_ge(s_rel, 16)
                pool.tensor_scalar(ext[:, :, 0:flat], rel[:, :, 0:1].to_broadcast([P, 8, flat]), 8.0, 1.0,
                                   ALU.mult, ALU.mult).then_inc(s_ext, 1)
                pool.tensor_scalar(ext[:, :, flat:EXT], rel[:, :, 0:EXT - flat], 8.0, 1.0,
                                   ALU.mult, ALU.mult).then_inc(s_ext, 1)
                pool.wait_ge(s_in, 48)
                pool.memset(band[0:CHUNK, :, B_WIN * P - CHUNK:], NEG).then_inc(s_mask, 1)
                pool.memset(band[CHUNK:P, :, 0:CHUNK], NEG).then_inc(s_mask, 1)

            n_dve = 5 + 3 + 4 + 5

            @block.scalar
            def _(act):
                act.wait_ge(s_v, n_dve)
                act.activation(sin[:, :], ang[:, :], ACT.Sin).then_inc(s_act, 1)
                act.activation(cos[:, :], turns[:, :], ACT.Sin).then_inc(s_act, 1)


def stage_memory(nc, mem, g_mem, w_k, w_v, kx_d, vx_d):
    with ExitStack() as ctx:
        room = Room(nc, ctx, "mem")
        norm = Norm(room)
        ident = room.sb("ident", [P, P])
        m_hi = room.sb("m_hi", [P, KT, MEM], F32R)
        m_lo = room.sb("m_lo", [P, KT, MEM], F32R)
        N_K, N_V, VW = KT, 4, 256
        w_raw = room.sb("w_raw", [P, 3, KT * VW])
        w_hi = room.sb("w_hi", [P, 2, KT * VW], F32R)
        w_lo = room.sb("w_lo", [P, 2, KT * VW], F32R)
        k_out = room.sb("k_out", [P, 2, N_K, MEM], F32R)
        v_out = room.sb("v_out", [P, 2, MT, D], F32R)
        acc = [room.bank(f"acc{i}") for i in range(2)]
        s_ident = room.sem("s_ident")
        s_w = [room.sem(f"s_w{i}") for i in range(3)]
        s_hi = room.sem("s_w_hi")
        s_lo = room.sem("s_w_lo")
        s_acc = room.sem("s_acc")
        s_ohi = room.sem("s_out_hi")
        s_olo = room.sem("s_out_lo")
        s_out = room.sem("s_out")
        items = [("k", m, KT * P) for m in range(N_K)] + [("v", c, KT * VW) for c in range(N_V)]
        accs = [(kind, m, t) for kind, m, _ in items for t in (range(1) if kind == "k" else range(MT))]

        acc_end = [sum(1 if kind == "k" else MT for kind, _, _ in items[:n + 1])
                   for n in range(len(items))]

        def target(kind, m, t, part):
            if kind == "k":
                return k_out[:, part, m, :]
            return v_out[:, part, t, m * VW:(m + 1) * VW]

        with nc.Block() as block:
            @block.sync
            def _(sp):
                for j in range(MT):
                    sp.dma_start(norm.x[:, j, :], mem[j * P:(j + 1) * P, :]).then_inc(norm.s_x[j], 16)
                sp.dma_start(norm.gain[:, :], g_mem.to_broadcast([P, D])).then_inc(norm.s_gain, 16)
                for n, (kind, m, w) in enumerate(items):
                    if n >= 3:
                        sp.wait_ge(s_lo, n - 2)
                    src = w_k[m] if kind == "k" else w_v[m]
                    sp.dma_start(w_raw[:, n % 3, 0:w], src).then_inc(s_w[n % 3], 16)
                sp.wait_ge(s_olo, len(accs))
                for part in range(2):
                    sp.dma_start(kx_d[part], raw(k_out[:, part, :, :].rearrange("p m t -> p (m t)"))).then_inc(s_out, 16)
                    sp.dma_start(vx_d[part], raw(v_out[:, part, :, :].rearrange("p t d -> p (t d)"))).then_inc(s_out, 16)
                sp.wait_ge(s_out, 64)

            @block.gpsimd
            def _(pool):
                make_identity(room, pool, ident, s_ident)
                norm.start_pool(pool)
                for n in range(MT):
                    norm.pool_rsqrt(pool, n, n)
                for n, (kind, m, w) in enumerate(items):
                    pool.wait_ge(s_hi, n + 1)
                    pool.tensor_tensor(w_lo[:, n % 2, 0:w], w_raw[:, n % 3, 0:w], raw(w_hi[:, n % 2, 0:w]),
                                       ALU.subtract).then_inc(s_lo, 1)

            @block.scalar
            def _(act):
                norm.start_act(act)
                for n in range(MT):
                    norm.act_square(act, n, n, 0)
                for n in range(MT):
                    for b in range(2):
                        norm.act_hi(act, n, b, m_hi[:, 4 * b:4 * b + 4, n * P:(n + 1) * P])
                for a, (kind, m, t) in enumerate(accs):
                    act.wait_ge(s_acc, a + 1)
                    act.activation(target(kind, m, t, 0), acc[a % 2][:, 0:VW], ACT.Copy).then_inc(s_ohi, 1)

            @block.vector
            def _(dve):
                norm.start_dve(dve)
                for n in range(MT):
                    norm.dve_scale(dve, n, n)
                for n in range(MT):
                    for b in range(2):
                        norm.dve_lo(dve, n, b, m_lo[:, 4 * b:4 * b + 4, n * P:(n + 1) * P],
                                    m_hi[:, 4 * b:4 * b + 4, n * P:(n + 1) * P])

                def w_high(n):
                    kind, m, w = items[n]
                    dve.wait_ge(s_w[n % 3], 16 * (n // 3) + 16)
                    if n >= 2:
                        dve.wait_ge(s_acc, acc_end[n - 2])
                    dve.tensor_copy(w_hi[:, n % 2, 0:w], w_raw[:, n % 3, 0:w]).then_inc(s_hi, 1)

                w_high(0)
                w_high(1)
                a = 0
                for n, (kind, m, w) in enumerate(items):
                    for t in (range(1) if kind == "k" else range(MT)):
                        dve.wait_ge(s_ohi, a + 1)
                        dve.tensor_tensor(target(kind, m, t, 1), acc[a % 2][:, 0:VW],
                                          raw(target(kind, m, t, 0)), ALU.subtract).then_inc(s_olo, 1)
                        a += 1
                    if n + 2 < len(items):
                        w_high(n + 2)

            @block.tensor
            def _(pe):
                norm.start_pe(pe)
                pe.wait_ge(s_ident, 2)
                for n in range(MT):
                    norm.pe_turn(pe, ident[:, :], n, n)
                pe.wait_ge(norm.s_lo, 2 * MT + RING)
                a = 0
                for n, (kind, m, w) in enumerate(items):
                    pe.wait_ge(s_lo, n + 1)
                    hi = w_hi[:, n % 2, 0:w].rearrange("p (k c) -> p k c", k=KT)
                    lo = w_lo[:, n % 2, 0:w].rearrange("p (k c) -> p k c", k=KT)
                    for t in (range(1) if kind == "k" else range(MT)):
                        if a >= 2:
                            pe.wait_ge(s_olo, a - 1)
                        for k in range(KT):
                            if kind == "k":
                                last = split3(pe, acc[a % 2][:, 0:MEM], hi[:, k, :], lo[:, k, :],
                                              m_hi[:, k, :], m_lo[:, k, :], k == 0, k == KT - 1)
                            else:
                                tok = slice(t * P, (t + 1) * P)
                                last = split3(pe, acc[a % 2][:, 0:VW], m_hi[:, k, tok], m_lo[:, k, tok],
                                              hi[:, k, :], lo[:, k, :], k == 0, k == KT - 1)
                        last.then_inc(s_acc, 1)
                        a += 1


def stage_qkv(nc, x, g_mix, w_qk, b_qk, w_v, b_v, cos_d, sin_d, qk_d, v_d):
    with ExitStack() as ctx:
        room = Room(nc, ctx, "qkv")
        norm = Norm(room)
        ident = room.sb("ident", [P, P])
        h_hi = room.sb("h_hi", [P, KT, HALF], F32R)
        h_lo = room.sb("h_lo", [P, KT, HALF], F32R)
        W_COLS = KT * V_GROUP
        w_raw = room.sb("w_raw", [P, 2, W_COLS])
        w_hi = room.sb("w_hi", [P, 2, W_COLS], F32R)
        w_lo = room.sb("w_lo", [P, 2, W_COLS], F32R)
        bias = room.sb("bias", [P, N_QK])
        bias_v = room.sb("bias_v", [P, 2 * V_GROUP])
        cos = room.sb("cos", [P, SEQ])
        sin = room.sb("sin", [P, SEQ])
        y = room.sb("y", [P, 2, HALF])
        swapped = room.sb("swapped", [P, HALF])
        cos_part = room.sb("cos_part", [P, HALF])
        o_hi = room.sb("o_hi", [P, 2, HALF], F32R)
        o_lo = room.sb("o_lo", [P, 2, HALF], F32R)
        acc = [room.bank(f"acc{i}") for i in range(4)]
        s_ident = room.sem("s_ident")
        s_const = room.sem("s_const")
        s_w = [room.sem(f"s_w{j}") for j in range(2)]
        s_whi = room.sem("s_w_hi")
        s_wlo = room.sem("s_w_lo")
        s_acc = room.sem("s_acc")
        s_read = room.sem("s_acc_read")
        s_swap = room.sem("s_swapped")
        s_cos = room.sem("s_products")
        s_y = room.sem("s_y")
        s_ohi = room.sem("s_out_hi")
        s_olo = room.sem("s_out_lo")
        s_st = [room.sem(f"s_stored{j}") for j in range(2)]

        BLK = HALF // BANK
        ITEMS = N_QK + 2
        USES = N_QK * BLK + 2 * HT
        OUTS = N_QK + 2 * HT
        EARLY = 16

        def blocks():
            return [(0, N_QK_A // 2, True), (N_QK_A // 2, (N_QK - N_QK_A) // 2, False)]

        with nc.Block() as block:
            @block.sync
            def _(sp):
                def load_x(hf, i, j):
                    n = hf * HT + i * 2 + j
                    sp.wait_ge(norm.s_xn, free(n))
                    sp.dma_start(norm.x[:, j, :], x[bass.ds(n * P, P), :]).then_inc(norm.s_x[j], 16)

                def load_w(hf, i, j):
                    m = i * 2 + j
                    sp.wait_ge(s_wlo, free(hf * ITEMS + m))
                    sp.dma_start(w_raw[:, j, 0:KT * P],
                                 w_qk[bass.ds(m, 1), :, :].rearrange("a p c -> p (a c)")).then_inc(s_w[j], 16)

                sp.dma_start(norm.gain[:, :], g_mix.to_broadcast([P, D])).then_inc(norm.s_gain, 16)
                sp.dma_start(bias[:, :], b_qk).then_inc(s_const, 16)
                sp.dma_start(bias_v[:, :], b_v.to_broadcast([P, 2 * V_GROUP])).then_inc(s_const, 16)
                sp.dma_start(cos[:, :], cos_d).then_inc(s_const, 16)
                sp.dma_start(sin[:, :], sin_d).then_inc(s_const, 16)
                with sp.Fori(0, 2) as hf:
                    with sp.Fori(0, HT // 2) as i:
                        for j in range(2):
                            load_x(hf, i, j)
                    with sp.Fori(0, N_QK // 2) as i:
                        for j in range(2):
                            load_w(hf, i, j)
                    for j in range(2):
                        sp.wait_ge(s_wlo, free(hf * ITEMS + N_QK + j))
                        sp.dma_start(w_raw[:, j, :], w_v[j]).then_inc(s_w[j], 16)

            @block.gpsimd
            def _(pool):
                make_identity(room, pool, ident, s_ident)
                norm.start_pool(pool)
                pool.sem_inc(s_wlo, RING)

                def split(n, j, use, used, w):
                    pool.wait_ge(s_w[j], 16 * use + 16)
                    pool.wait_ge(s_acc, used)
                    room.gate(pool)
                    pool.tensor_scalar(w_hi[:, j, 0:w], w_raw[:, j, 0:w], 1.0, 1.0,
                                       ALU.mult, ALU.mult).then_inc(s_whi, 1)
                    pool.wait_ge(s_whi, n + 1)
                    pool.tensor_tensor(w_lo[:, j, 0:w], w_raw[:, j, 0:w], raw(w_hi[:, j, 0:w]),
                                       ALU.subtract).then_inc(s_wlo, 1)

                with pool.Fori(0, 2) as hf:
                    with pool.Fori(0, HT // 2) as i:
                        for j in range(2):
                            norm.pool_rsqrt(pool, hf * HT + i * 2 + j, j)
                    for j in range(2):
                        split(hf * ITEMS + j, j, hf * (ITEMS // 2), hf * USES + EARLY - HT * (1 - j), KT * P)
                    with pool.Fori(1, N_QK // 2) as i:
                        for j in range(2):
                            split(hf * ITEMS + i * 2 + j, j, hf * (ITEMS // 2) + i,
                                  hf * USES + (i * 2 + j - 1) * BLK + EARLY, KT * P)
                    for j in range(2):
                        split(hf * ITEMS + N_QK + j, j, hf * (ITEMS // 2) + N_QK // 2,
                              hf * USES + (N_QK + j - 1) * BLK + EARLY, W_COLS)

            @block.scalar
            def _(act):
                norm.start_act(act)

                def high(j, use, w, s_there, there):
                    act.wait_ge(s_st[j], 32 * use)
                    act.wait_ge(s_there, there)
                    act.activation(o_hi[:, j, 0:w], y[:, j, 0:w], ACT.Copy).then_inc(s_ohi, 1)

                def store(o, j, hi_at, lo_at, w):
                    act.wait_ge(s_ohi, o + 1)
                    act.dma_start(hi_at, raw(o_hi[:, j, 0:w])).then_inc(s_st[j], 16)
                    act.wait_ge(s_olo, made(o))
                    act.dma_start(lo_at, raw(o_lo[:, j, 0:w])).then_inc(s_st[j], 16)

                def qk_at(part, m, hf):
                    return qk_d[part, bass.ds(m, 1), :, bass.ds(hf * HALF, HALF)].rearrange("a p t -> p (a t)")

                with act.Fori(0, 2) as hf:
                    with act.Fori(0, HT // 2) as i:
                        for j in range(2):
                            norm.act_square(act, hf * HT + i * 2 + j, j, hf * (HT // 2) + i)
                        for j in range(2):
                            for b in range(2):
                                act.wait_ge(norm.s_turned, 2 * (hf * HT + i * 2 + j) + b + 1 + 2 * RING)
                                room.gate(act)
                                tok = bass.ds(i * (2 * P) + j * P, P)
                                act.activation(h_hi[:, 4 * b:4 * b + 4, tok],
                                               norm.turned[b][:, :].rearrange("p (k t) -> p k t", k=4),
                                               ACT.Copy).then_inc(norm.s_hi, 1)
                    for first, pairs, rotated in blocks():
                        with act.Fori(first, first + pairs) as i:
                            for j in range(2):
                                m = i * 2 + j
                                o = hf * OUTS + m
                                biased = hf * USES + m * BLK + BLK + 4
                                if rotated:
                                    act.wait_ge(s_read, biased)
                                    act.wait_ge(s_y, hf * N_QK_A + m)
                                    for head in (0, HD):
                                        for a, b in ((0, HD // 2), (HD // 2, 0)):
                                            act.dma_start(swapped[head + a:head + a + HD // 2, :],
                                                          y[head + b:head + b + HD // 2, j, :]).then_inc(s_swap, 16)
                                if rotated:
                                    high(j, hf * (OUTS // 2) + i, HALF, s_y, hf * N_QK_A + m + 1)
                                else:
                                    high(j, hf * (OUTS // 2) + i, HALF, s_read, biased)
                                store(o, j, qk_at(0, m, hf), qk_at(1, m, hf), HALF)
                    for g in range(2):
                        with act.Fori(0, HT // 2) as i:
                            for j in range(2):
                                o = hf * OUTS + N_QK + g * HT + i * 2 + j
                                biased = hf * USES + N_QK * BLK + g * HT + i * 2 + j + 1 + 4
                                high(j, hf * (OUTS // 2) + N_QK // 2 + g * (HT // 2) + i, V_GROUP, s_read, biased)
                                rows = bass.ds(hf * HALF + i * (2 * P) + j * P, P)
                                cols = slice(g * V_GROUP, (g + 1) * V_GROUP)
                                store(o, j, v_d[0, rows, cols], v_d[1, rows, cols], V_GROUP)
                for j in range(2):
                    act.wait_ge(s_st[j], 32 * OUTS)

            @block.vector
            def _(dve):
                norm.start_dve(dve)
                dve.sem_inc(s_read, 4)
                dve.sem_inc(s_olo, RING)
                dve.wait_ge(s_const, 64)

                def low(o, j, w):
                    dve.wait_ge(s_ohi, o + 1)
                    dve.tensor_tensor(o_lo[:, j, 0:w], y[:, j, 0:w], raw(o_hi[:, j, 0:w]),
                                      ALU.subtract).then_inc(s_olo, 1)

                with dve.Fori(0, 2) as hf:
                    with dve.Fori(0, HT // 2) as i:
                        for j in range(2):
                            norm.dve_scale(dve, hf * HT + i * 2 + j, j)
                        for j in range(2):
                            tok = bass.ds(i * (2 * P) + j * P, P)
                            for b in range(2):
                                norm.dve_lo(dve, hf * HT + i * 2 + j, b, h_lo[:, 4 * b:4 * b + 4, tok],
                                            h_hi[:, 4 * b:4 * b + 4, tok])
                    for first, pairs, rotated in blocks():
                        with dve.Fori(first, first + pairs) as i:
                            for j in range(2):
                                m = i * 2 + j
                                o = hf * OUTS + m
                                dve.wait_ge(s_olo, free(o))
                                for b in range(BLK):
                                    dve.wait_ge(s_acc, hf * USES + m * BLK + b + 1 + EARLY)
                                    last = dve.tensor_scalar(y[:, j, b * BANK:(b + 1) * BANK],
                                                             acc[j * BLK + b][:, :], bias[:, bass.ds(m, 1)],
                                                             None, ALU.add)
                                    last.then_inc(s_read, 1)
                                here = slice(0, HALF)
                                dve.wait_ge(s_read, hf * USES + m * BLK + BLK + 4)
                                if rotated:
                                    r = hf * N_QK_A + m
                                    table = bass.ds(hf * HALF, HALF)
                                    dve.wait_ge(s_y, r)
                                    dve.tensor_tensor(cos_part[:, :], y[:, j, here], cos[:, table],
                                                      ALU.mult).then_inc(s_cos, 1)
                                    dve.wait_ge(s_swap, 64 * r + 64)
                                    dve.tensor_tensor(swapped[:, :], swapped[:, :], sin[:, table],
                                                      ALU.mult).then_inc(s_cos, 1)
                                    dve.wait_ge(s_cos, 2 * r + 2)
                                    dve.tensor_tensor(y[:, j, here], cos_part[:, :], swapped[:, :],
                                                      ALU.add).then_inc(s_y, 1)
                                low(o, j, HALF)
                    for g in range(2):
                        with dve.Fori(0, HT // 4) as i:
                            for q in range(4):
                                tt = i * 4 + q
                                o = hf * OUTS + N_QK + g * HT + tt
                                a = hf * USES + N_QK * BLK + g * HT + tt
                                dve.wait_ge(s_olo, free(o))
                                dve.wait_ge(s_acc, a + 1 + EARLY)
                                dve.tensor_tensor(y[:, q % 2, 0:V_GROUP], acc[q][:, 0:V_GROUP],
                                                  bias_v[:, g * V_GROUP:(g + 1) * V_GROUP],
                                                  ALU.add).then_inc(s_read, 1)
                                low(o, q % 2, V_GROUP)

            @block.tensor
            def _(pe):
                norm.start_pe(pe)
                pe.sem_inc(s_acc, EARLY)
                pe.wait_ge(s_ident, 2)
                with pe.Fori(0, 2) as hf:
                    with pe.Fori(0, HT // 2) as i:
                        for j in range(2):
                            norm.pe_turn(pe, ident[:, :], hf * HT + i * 2 + j, j)
                    pe.wait_ge(norm.s_lo, hf * (2 * HT) + 2 * HT + RING)
                    room.gate(pe)
                    with pe.Fori(0, N_QK // 2) as i:
                        for j in range(2):
                            m = i * 2 + j
                            pe.wait_ge(s_wlo, made(hf * ITEMS + m))
                            for b in range(BLK):
                                a = hf * USES + m * BLK + b
                                pe.wait_ge(s_read, a + 1)
                                cols = slice(b * BANK, (b + 1) * BANK)
                                for k in range(KT):
                                    wk = slice(k * P, (k + 1) * P)
                                    last = split3(pe, acc[j * BLK + b][:, :], w_hi[:, j, wk], w_lo[:, j, wk],
                                                  h_hi[:, k, cols], h_lo[:, k, cols], k == 0, k == KT - 1)
                                last.then_inc(s_acc, 1)
                    for g in range(2):
                        pe.wait_ge(s_wlo, made(hf * ITEMS + N_QK + g))
                        for tt in range(HT):
                            a = hf * USES + N_QK * BLK + g * HT + tt
                            pe.wait_ge(s_read, a + 1)
                            tok = slice(tt * P, (tt + 1) * P)
                            for k in range(KT):
                                wk = slice(k * V_GROUP, (k + 1) * V_GROUP)
                                last = split3(pe, acc[tt % 4][:, 0:V_GROUP], h_hi[:, k, tok], h_lo[:, k, tok],
                                              w_hi[:, g, wk], w_lo[:, g, wk], k == 0, k == KT - 1)
                            last.then_inc(s_acc, 1)


def stage_attention(nc, group, qk_d, v_d, mix_d, bias_d, sinks8):
    is_a = group == "a"
    win = A_WIN if is_a else B_WIN
    bodies, pairs = (1, N_PAIR) if is_a else (2, 2)
    heads = 2 if is_a else 1
    q0, k0 = (0, 4) if is_a else (N_QK_A, N_QK_A + 4)
    vw = HD if is_a else P
    v0 = 0 if is_a else A_KV
    skip = CHUNK if is_a else 0

    units = [(pp, i, h) for pp in range(pairs) for h in range(0, 2, heads) for i in range(NT)]
    NB = len(units)

    def tiles(i):
        return min(i + 1, win)

    def pieces(i):
        w = tiles(i)
        if is_a or w == 1:
            return [(0, w)]
        return [(0, (w + 1) // 2), ((w + 1) // 2, w)]

    starts = [0]
    for _, i, _ in units:
        starts.append(starts[-1] + len(pieces(i)))
    NPC = starts[-1]
    assert NPC % 2 == 0 and NB % 4 == 0

    with ExitStack() as ctx:
        room = Room(nc, ctx, f"att_{group}")
        ident = room.sb("ident", [P, P])
        q_t = [room.sb(f"q{part}", [P, 2, SEQ], F32R) for part in range(2)]
        k_t = [room.sb(f"k{part}", [P, 2, SEQ], F32R) for part in range(2)]
        v_t = [room.sb(f"v{part}", [P, 2, NT, vw], F32R) for part in range(2)]
        SW = heads * win * P
        bias = room.sb("bias", [P, 2, win * P] if is_a else [P, 2, 2, win * P])
        sink = room.sb("sink", [P, 8])
        scores = room.sb("scores", [P, 2, SW])
        probs = room.sb("probs", [P, 2, SW])
        t_hi = room.sb("t_hi", [P, 2, SW], F32R)
        t_lo = room.sb("t_lo", [P, 2, SW], F32R)
        top = room.sb("top", [P, 4, heads])
        minus = room.sb("minus", [P, 4, heads])
        total = room.sb("total", [P, 4, heads])
        rest = room.sb("rest", [P, 4, heads])
        whole = room.sb("whole", [P, 4, heads])
        part_of = room.sb("part_of", [P, 4, heads])
        rest2 = room.sb("rest2", [P, 4, heads])
        out = room.sb("out", [P, 2, NT, P])
        sum_s = [room.bank(f"sum_s{j}", 2) for j in range(2)]
        turned = [room.bank(f"turned{j}") for j in range(2)]
        sum_o = [room.bank(f"sum_o{j}") for j in range(2)]
        s_ident = room.sem("s_ident")
        s_const = room.sem("s_const")
        s_ld = [room.sem(f"s_ld{j}") for j in range(2)]
        s_bias = [room.sem(f"s_bias{j}") for j in range(2)]
        s_s = room.sem("s_scores")
        s_max = room.sem("s_max")
        s_minus = room.sem("s_minus")
        s_exp = room.sem("s_exp")
        s_rest = room.sem("s_rest")
        s_t = room.sem("s_turned")
        s_hi = room.sem("s_hi")
        s_lo = room.sem("s_lo")
        s_o = room.sem("s_o")
        s_den = room.sem("s_den")
        s_out = room.sem("s_out")
        s_st = [room.sem(f"s_st{j}") for j in range(2)]
        s_zero = room.sem("s_zero")

        def body(engine):
            return engine.Fori(0, bodies) if bodies > 1 else nullcontext(0)

        per_pair = NB // pairs
        EARLY = per_pair

        with nc.Block() as block:
            @block.sync
            def _(sp):
                if is_a:
                    sp.dma_start(sink[:, :], sinks8.to_broadcast([P, 8])).then_inc(s_const, 16)
                with body(sp) as g:
                    for pp in range(pairs):
                        j = pp % 2
                        sp.wait_ge(s_o, g * NB + (pp - 1) * per_pair + EARLY)
                        for part in range(2):
                            at = q0 + pp if is_a else bass.ds(q0 + g * pairs + pp, 1)
                            src = qk_d[part, at, :, :] if is_a else qk_d[part, at, :, :].rearrange("a p t -> p (a t)")
                            sp.dma_start(raw(q_t[part][:, j, :]), src).then_inc(s_ld[j], 16)
                            if is_a and pp % 2 == 0:
                                kv = pp // 2
                                sp.dma_start(raw(k_t[part][:, kv, :]), qk_d[part, k0 + kv, :, :]).then_inc(s_ld[j], 16)
                                sp.dma_start(raw(v_t[part][:, kv, :, :]),
                                             v_d[part, :, kv * HD:(kv + 1) * HD].rearrange("(i p) c -> p i c", p=P)
                                             ).then_inc(s_ld[j], 16)
                            if not is_a:
                                at = bass.ds(k0 + g * pairs + pp, 1)
                                sp.dma_start(raw(k_t[part][:, j, :]),
                                             qk_d[part, at, :, :].rearrange("a p t -> p (a t)")).then_inc(s_ld[j], 16)
                                cols = bass.ds(g * (pairs * P) + (v0 + pp * P), P)
                                sp.dma_start(raw(v_t[part][:, j, :, :]),
                                             v_d[part, :, cols].rearrange("(i p) c -> p i c", p=P)).then_inc(s_ld[j], 16)
                        if not is_a:
                            sp.wait_ge(s_max, g * NB + (pp - 1) * per_pair + EARLY)
                            heads_at = bass.ds(g * (2 * pairs) + 2 * pp, 2)
                            sp.dma_start(bias[:, j, :, :], bias_d[heads_at, :, :].rearrange("h p n -> p h n")
                                         ).then_inc(s_bias[j], 16)

            def loaded(g, pp):
                return (96, 32, 192, 64)[pp] if is_a else g * 96 + 96

            @block.gpsimd
            def _(pool):
                make_identity(room, pool, ident, s_ident)
                pool.memset(probs[:, :, :], 0.0).then_inc(s_zero, 1)
                if is_a:
                    pool.memset(bias[:, :, :], 0.0).then_inc(s_zero, 1)
                    pool.wait_ge(s_zero, 2)
                    pool.memset(bias[0:CHUNK, 0, 3 * CHUNK:4 * CHUNK], NEG).then_inc(s_zero, 1)
                    pool.memset(bias[CHUNK:P, 0, CHUNK:2 * CHUNK], NEG).then_inc(s_zero, 1)
                with body(pool) as g:
                    for pp in range(pairs):
                        j = pp % 2
                        pool.wait_ge(s_out, g * NB + (pp + 1) * per_pair + 4)
                        cols0 = (0 if is_a else A_Q) + pp * P
                        cols = slice(cols0, cols0 + P) if is_a else bass.ds(g * (pairs * P) + cols0, P)
                        pool.dma_start(mix_d[:, cols].rearrange("(i p) c -> p i c", p=P),
                                       out[:, j, :, :]).then_inc(s_st[j], 16)
                for j in range(2):
                    pool.wait_ge(s_st[j], 16 * bodies * pairs // 2)

            @block.scalar
            def _(act):
                act.sem_inc(s_exp, RING)
                act.wait_ge(s_zero, 4 if is_a else 1)

                def high(g, u):
                    pp, i, h = units[u]
                    act.wait_ge(s_o, g * NB + u - 1 + EARLY)
                    for piece, (a, b) in enumerate(pieces(i)):
                        c = starts[u] + piece
                        act.wait_ge(s_t, g * NPC + c + 1 + 4)
                        cols = slice(a * P * heads, b * P * heads)
                        act.activation(t_hi[:, u % 2, cols], turned[c % 2][:, 0:(b - a) * P * heads],
                                       ACT.Copy).then_inc(s_hi, 1)

                def exps(g, u):
                    pp, i, h = units[u]
                    act.wait_ge(s_minus, g * NB + u + 1)
                    act.wait_ge(s_t, g * NPC + (starts[u - 1] if u >= 2 else starts[NB + u - 1] - NPC) + 4)
                    w = tiles(i) * P - (skip if tiles(i) == win else 0)
                    for x in range(heads):
                        last = act.activation(probs[:, u % 2, (x + 1) * win * P - w:(x + 1) * win * P],
                                              scores[:, u % 2, x * win * P:x * win * P + w], ACT.Exp,
                                              bias=minus[:, u % 4, x:x + 1], scale=0.125,
                                              accum_out=total[:, u % 4, x:x + 1])
                    if is_a:
                        last = act.activation(whole[:, u % 4, :], rest[:, u % 4, :], ACT.Exp, scale=0.125)
                    last.then_inc(s_exp, 1)

                with body(act) as g:
                    for step in range(NB + 1):
                        if step >= 1:
                            high(g, step - 1)
                        if step < NB:
                            exps(g, step)

            @block.vector
            def _(dve):
                dve.sem_inc(s_max, EARLY)
                dve.sem_inc(s_lo, RING)
                dve.sem_inc(s_out, 4)
                if is_a:
                    dve.wait_ge(s_const, 16)
                    dve.tensor_scalar(sink[:, :], sink[:, :], 8.0, None, ALU.mult).then_inc(s_rest, 1)
                    dve.wait_ge(s_rest, 1)
                    dve.wait_ge(s_zero, 4)

                def maxima(g, u):
                    pp, i, h = units[u]
                    n = g * NB + u
                    w = tiles(i) * P - (skip if tiles(i) == win else 0)
                    if not is_a and u % per_pair == 0:
                        dve.wait_ge(s_bias[pp % 2], g * 16 + 16)
                    dve.wait_ge(s_exp, n + 1)
                    dve.wait_ge(s_s, n + 1)
                    room.gate(dve)
                    for x in range(heads):
                        head = pp * 2 + h + x
                        if is_a:
                            add = bias[:, 0, win * P - w:win * P]
                            start = sink[:, head:head + 1]
                        else:
                            add = bias[:, pp % 2, h, win * P - w:win * P]
                            start = -3e38
                        last = dve.tensor_tensor_reduce(
                            out=scores[:, u % 2, x * win * P:x * win * P + w],
                            in0=sum_s[u % 2][:, x * BANK:x * BANK + w],
                            in1=add, scale=1.0, scalar=start, op0=ALU.add, op1=ALU.max,
                            accum_out=top[:, u % 4, x:x + 1])
                    last.then_inc(s_max, 1)
                    dve.wait_ge(s_max, n + 1 + EARLY)
                    last = dve.tensor_scalar(minus[:, u % 4, :], top[:, u % 4, :], -0.125, None, ALU.mult)
                    if is_a:
                        first = pp * 2
                        last = dve.tensor_tensor(rest[:, u % 4, :], sink[:, first:first + 2], top[:, u % 4, :],
                                                 ALU.subtract)
                    last.then_inc(s_minus, 1)

                def low(g, u):
                    pp, i, h = units[u]
                    for piece, (a, b) in enumerate(pieces(i)):
                        c = starts[u] + piece
                        dve.wait_ge(s_hi, g * NPC + c + 1)
                        cols = slice(a * P * heads, b * P * heads)
                        dve.tensor_tensor(t_lo[:, u % 2, cols], turned[c % 2][:, 0:(b - a) * P * heads],
                                          raw(t_hi[:, u % 2, cols]), ALU.subtract).then_inc(s_lo, 1)

                def divide(g, u):
                    pp, i, h = units[u]
                    n = g * NB + u
                    j = pp % 2
                    denominator = total[:, u % 4, :]
                    steps = 2 if is_a else 1
                    if is_a:
                        dve.tensor_tensor(part_of[:, u % 4, :], total[:, u % 4, :], whole[:, u % 4, :],
                                          ALU.add).then_inc(s_den, 1)
                        dve.wait_ge(s_den, n * steps + 1)
                        denominator = part_of[:, u % 4, :]
                    dve.reciprocal(rest2[:, u % 4, :], denominator).then_inc(s_den, 1)
                    dve.wait_ge(s_o, n + 1 + EARLY)
                    if u % per_pair == 0:
                        dve.wait_ge(s_st[j], 16 * (pp // 2) if is_a else g * 16)
                    dve.wait_ge(s_den, n * steps + steps)
                    at = out[:, j, i, h * HD:(h + heads) * HD].rearrange("p (h c) -> p h c", h=heads)
                    dve.tensor_tensor(at, sum_o[u % 2][:, 0:heads * HD].rearrange("p (h c) -> p h c", h=heads),
                                      rest2[:, u % 4, :].unsqueeze(2).to_broadcast([P, heads, HD]),
                                      ALU.mult).then_inc(s_out, 1)

                with body(dve) as g:
                    for step in range(NB + 2):
                        if step < NB:
                            maxima(g, step)
                        if 1 <= step <= NB:
                            low(g, step - 1)
                        if step >= 2:
                            divide(g, step - 2)

            @block.tensor
            def _(pe):
                pe.sem_inc(s_t, 4)
                pe.sem_inc(s_o, EARLY)
                pe.wait_ge(s_ident, 2)

                def score(g, u):
                    pp, i, h = units[u]
                    n = g * NB + u
                    if u % per_pair == 0:
                        pe.wait_ge(s_ld[pp % 2], loaded(g, pp))
                    pe.wait_ge(s_max, n - 1 + EARLY)
                    full = tiles(i) == win
                    key0 = (i + 1 - tiles(i)) * P + (skip if full else 0)
                    w = (i + 1) * P - key0
                    ks = (pp // 2) if is_a else pp % 2
                    for x in range(heads):
                        rows = slice((h + x) * HD, (h + x + 1) * HD)
                        qs = slice(i * P, (i + 1) * P)
                        for a in range(0, w, BANK):
                            b = min(a + BANK, w)
                            cols = slice(key0 + a, key0 + b)
                            base = x * BANK
                            last = split3(pe, sum_s[u % 2][:, base + a:base + b],
                                          q_t[0][rows, pp % 2, qs], q_t[1][rows, pp % 2, qs],
                                          k_t[0][rows, ks, cols], k_t[1][rows, ks, cols], True, True)
                    last.then_inc(s_s, 1)

                def turn(g, u):
                    pp, i, h = units[u]
                    n = g * NB + u
                    pe.wait_ge(s_exp, n + 1 + RING)
                    for piece, (a, b) in enumerate(pieces(i)):
                        c = starts[u] + piece
                        pe.wait_ge(s_lo, g * NPC + c + 1)
                        blocks = [(x, y) for x in range(heads) for y in range(a, b)]
                        for z, (x, y) in enumerate(blocks):
                            at = slice(z * P, (z + 1) * P)
                            end = (x + 1) * win - tiles(i) + y + 1
                            src = slice((end - 1) * P, end * P)
                            last = pe.transpose(turned[c % 2][:, at], probs[:, u % 2, src], ident[:, :])
                        last.then_inc(s_t, 1)

                def values(g, u):
                    pp, i, h = units[u]
                    n = g * NB + u
                    pe.wait_ge(s_lo, g * NPC + starts[u + 1] + RING)
                    pe.wait_ge(s_out, n + 1 + RING)
                    w = tiles(i)
                    vs = (pp // 2) if is_a else pp % 2
                    for x in range(heads):
                        cols = slice(0, HD) if is_a else slice(h * HD, (h + 1) * HD)
                        for y in range(w):
                            kt = i + 1 - w + y
                            at = slice((x * w + y) * P, (x * w + y + 1) * P)
                            last = split3(pe, sum_o[u % 2][:, x * HD:(x + 1) * HD],
                                          t_hi[:, u % 2, at], t_lo[:, u % 2, at],
                                          v_t[0][:, vs, kt, cols], v_t[1][:, vs, kt, cols], y == 0, y == w - 1)
                    last.then_inc(s_o, 1)

                with body(pe) as g:
                    for step in range(NB + 2):
                        if step < NB:
                            score(g, step)
                        if 1 <= step <= NB:
                            turn(g, step - 1)
                        if step >= 2:
                            values(g, step - 2)


class Resident:

    def __init__(self, room, name, weight, stage=None):
        self.weight = weight
        self.stage = room.sb(f"{name}_raw", [P, 2, D]) if stage is None else stage
        self.hi = room.sb(f"{name}_hi", [P, KT, D], F32R)
        self.lo = room.sb(f"{name}_lo", [P, KT, D], F32R)
        self.s_in = [room.sem(f"s_{name}_in{j}") for j in range(2)]
        self.s_hi = room.sem(f"s_{name}_hi")
        self.s_lo = room.sem(f"s_{name}_lo")

    def load(self, sp):
        for k in range(KT):
            if k >= 2:
                sp.wait_ge(self.s_lo, k - 1)
            sp.dma_start(self.stage[:, k % 2, :], self.weight[k]).then_inc(self.s_in[k % 2], 16)

    def high(self, act):
        for k in range(KT):
            act.wait_ge(self.s_in[k % 2], 16 * (k // 2) + 16)
            act.activation(self.hi[:, k, :], self.stage[:, k % 2, :], ACT.Copy).then_inc(self.s_hi, 1)

    def low(self, dve):
        for k in range(KT):
            dve.wait_ge(self.s_hi, k + 1)
            dve.tensor_tensor(self.lo[:, k, :], self.stage[:, k % 2, :], raw(self.hi[:, k, :]),
                              ALU.subtract).then_inc(self.s_lo, 1)


def over_pairs(engine, pairs, body):
    with engine.Fori(0, pairs - 1) as i:
        body(i, True)
    body(pairs - 1, False)


def rows_of(tensor, n):
    return tensor[n * P:(n + 1) * P, :] if isinstance(n, int) else tensor[bass.ds(n * P, P), :]


def stage_mix(nc, mix_d, gain, x, w_out, x2_d):
    with ExitStack() as ctx:
        room = Room(nc, ctx, "mix")
        norm = Norm(room, groups=2)
        weight = Resident(room, "w", w_out)
        ident = room.sb("ident", [P, P])
        m_hi = room.sb("m_hi", [P, 2, KT, P], F32R)
        m_lo = room.sb("m_lo", [P, 2, KT, P], F32R)
        res = room.sb("res", [P, 2, D])
        out = room.sb("out", [P, 2, D])
        acc = [room.bank(f"acc{i}") for i in range(4)]
        s_ident = room.sem("s_ident")
        s_res = [room.sem(f"s_res{j}") for j in range(2)]
        s_acc = room.sem("s_acc")
        s_sum = room.sem("s_sum")
        s_st = [room.sem(f"s_st{j}") for j in range(2)]
        PAIRS = NT // 2

        with nc.Block() as block:
            @block.sync
            def _(sp):
                sp.dma_start(norm.gain[:, :], gain.to_broadcast([P, D])).then_inc(norm.s_gain, 16)
                for j in range(2):
                    sp.dma_start(norm.x[:, j, :], rows_of(mix_d, j)).then_inc(norm.s_x[j], 16)
                    sp.dma_start(res[:, j, :], rows_of(x, j)).then_inc(s_res[j], 16)
                weight.load(sp)

                def pair(i, more):
                    for j in range(2):
                        n = i * 2 + j
                        if more:
                            sp.wait_ge(norm.s_xn, made(n))
                            sp.dma_start(norm.x[:, j, :], rows_of(mix_d, n + 2)).then_inc(norm.s_x[j], 16)
                        sp.wait_ge(s_sum, n * 2 + 2 + 4)
                        sp.dma_start(rows_of(x2_d, n), out[:, j, :]).then_inc(s_st[j], 16)
                        if more:
                            sp.dma_start(res[:, j, :], rows_of(x, n + 2)).then_inc(s_res[j], 16)

                over_pairs(sp, PAIRS, pair)
                for j in range(2):
                    sp.wait_ge(s_st[j], 16 * PAIRS)

            @block.gpsimd
            def _(pool):
                make_identity(room, pool, ident, s_ident)
                norm.start_pool(pool)
                with pool.Fori(0, PAIRS) as i:
                    for j in range(2):
                        norm.pool_rsqrt(pool, i * 2 + j, j)

            @block.scalar
            def _(act):
                norm.start_act(act)

                def shape(n, j, use):
                    norm.act_square(act, n, j, use)
                    act.wait_ge(s_acc, n * 2 - 2 + 4)
                    for b in range(2):
                        norm.act_hi(act, n, b, m_hi[:, j, 4 * b:4 * b + 4, :])

                shape(0, 0, 0)
                weight.high(act)

                def pair(i, more):
                    shape(i * 2 + 1, 1, i)
                    if more:
                        shape(i * 2 + 2, 0, i + 1)

                over_pairs(act, PAIRS, pair)

            @block.vector
            def _(dve):
                norm.start_dve(dve)
                dve.sem_inc(s_sum, 4)

                def shape(n, j):
                    norm.dve_scale(dve, n, j)
                    for b in range(2):
                        norm.dve_lo(dve, n, b, m_lo[:, j, 4 * b:4 * b + 4, :], m_hi[:, j, 4 * b:4 * b + 4, :])

                shape(0, 0)
                weight.low(dve)

                def pair(i, more):
                    for j in range(2):
                        n = i * 2 + j
                        if more or j == 0:
                            shape(n + 1, (j + 1) % 2)
                        dve.wait_ge(s_res[j], 16 * i + 16)
                        dve.wait_ge(s_st[j], 16 * i)
                        for b in range(2):
                            cols = slice(b * BANK, (b + 1) * BANK)
                            dve.wait_ge(s_acc, n * 2 + b + 1 + 4)
                            dve.tensor_tensor(out[:, j, cols], acc[j * 2 + b][:, :], res[:, j, cols],
                                              ALU.add).then_inc(s_sum, 1)

                over_pairs(dve, PAIRS, pair)

            @block.tensor
            def _(pe):
                norm.start_pe(pe)
                pe.sem_inc(s_acc, 4)
                pe.wait_ge(s_ident, 2)
                norm.pe_turn(pe, ident[:, :], 0, 0)
                pe.wait_ge(weight.s_lo, KT)

                def pair(i, more):
                    for j in range(2):
                        n = i * 2 + j
                        pe.wait_ge(norm.s_lo, n * 2 + 2 + RING)
                        for b in range(2):
                            cols = slice(b * BANK, (b + 1) * BANK)
                            pe.wait_ge(s_sum, n * 2 + b + 1)
                            for k in range(KT):
                                last = split3(pe, acc[j * 2 + b][:, :], m_hi[:, j, k, :], m_lo[:, j, k, :],
                                              weight.hi[:, k, cols], weight.lo[:, k, cols],
                                              k == 0, k == KT - 1)
                            last.then_inc(s_acc, 1)
                            if b == 0 and (more or j == 0):
                                norm.pe_turn(pe, ident[:, :], n + 1, (j + 1) % 2)

                over_pairs(pe, PAIRS, pair)


def stage_cross(nc, x2_d, g_cross, w_cq, kx_d, vx_d, o_d):
    with ExitStack() as ctx:
        room = Room(nc, ctx, "cross")
        norm = Norm(room)
        BT = BANK // P
        NBLK = SEQ // BANK
        UNITS = XH * BT
        DT = XD // P
        ident = room.sb("ident", [P, P])
        h_hi = room.sb("h_hi", [P, KT, BANK], F32R)
        h_lo = room.sb("h_lo", [P, KT, BANK], F32R)
        q_hi = room.sb("q_hi", [P, KT, BANK], F32R)
        q_lo = room.sb("q_lo", [P, KT, BANK], F32R)
        k_p = [room.sb(f"k{part}", [P, KT, MEM], F32R) for part in range(2)]
        v_p = [room.sb(f"v{part}", [P, MT, D], F32R) for part in range(2)]
        probs = room.sb("probs", [P, 2, MEM])
        t_hi = room.sb("t_hi", [P, 2, MT, BANK], F32R)
        t_lo = room.sb("t_lo", [P, 2, MT, BANK], F32R)
        o_p = room.sb("o_p", [P, 2, 2 * BANK])
        o_hi = o_p[:, :, 0:BANK].bitcast(F32R)
        o_lo = o_p[:, :, BANK:2 * BANK].bitcast(F32R)
        weight = Resident(room, "w", w_cq, stage=o_p)
        top = room.sb("top", [P, 4])
        minus = room.sb("minus", [P, 4])
        total = room.sb("total", [P, 4])
        share = room.sb("share", [P, 4])
        sum_s = [room.bank(f"sum_s{j}") for j in range(2)]
        turned = room.bank("turned_p")
        sum_q = room.bank("sum_q")
        sum_o = [room.bank(f"sum_o{j}") for j in range(2)]
        s_ident = room.sem("s_ident")
        s_kv = room.sem("s_kv")
        s_s = room.sem("s_scores")
        s_max = room.sem("s_max")
        s_minus = room.sem("s_minus")
        s_exp = room.sem("s_exp")
        s_share = room.sem("s_share")
        s_p = room.sem("s_probs")
        s_t = room.sem("s_turned_p")
        s_thi = room.sem("s_turned_p_hi")
        s_tlo = room.sem("s_turned_p_lo")
        s_q = room.sem("s_q")
        s_qhi = room.sem("s_q_hi")
        s_qlo = room.sem("s_q_lo")
        s_o = room.sem("s_o")
        s_ohi = room.sem("s_o_hi")
        s_olo = room.sem("s_o_lo")
        s_st = [room.sem(f"s_st{j}") for j in range(2)]

        def events(more):
            order = []
            for u in range(UNITS):
                h, t = divmod(u, BT)
                order.append(("S", u))
                if more:
                    order += [("f", u)] * (u < BT) + [("g", u - 1)] * (1 <= u < BT + 1) \
                        + [("F", u - 2)] * (2 <= u < BT + 2) + [("Q", u - 6)] * (u >= 6)
                if u >= 2:
                    order.append(("T", u - 2))
                if h >= 1 and t == 2:
                    order.append(("O", h - 1))
            tail = [("T", UNITS - 2), ("Q", 10), ("T", UNITS - 1), ("Q", 11), ("Q", 12), ("O", XH - 1),
                    ("Q", 13), ("Q", 14), ("Q", 15)]
            return order + [e for e in tail if more or e[0] != "Q"]

        first = [(kind, t) for t in range(BT) for kind in "fgF"] + [("Q", x) for x in range(2 * KT)]

        def run(engine, do):
            for kind, x in first:
                if kind in do:
                    do[kind](-1, x)
            with engine.Fori(0, NBLK - 1) as b:
                for kind, x in events(True):
                    if kind in do:
                        do[kind](b, x)
            for kind, x in events(False):
                if kind in do:
                    do[kind](NBLK - 1, x)

        with nc.Block() as block:
            @block.sync
            def _(sp):
                sp.dma_start(norm.gain[:, :], g_cross.to_broadcast([P, D])).then_inc(norm.s_gain, 16)
                weight.load(sp)
                for part in range(2):
                    sp.dma_start(raw(k_p[part][:, :, :].rearrange("p k t -> p (k t)")), kx_d[part]).then_inc(s_kv, 16)
                    sp.dma_start(raw(v_p[part][:, :, :].rearrange("p k t -> p (k t)")), vx_d[part]).then_inc(s_kv, 16)

                def load(b, t):
                    n = b * BT + BT + t
                    sp.wait_ge(norm.s_xn, free(n))
                    sp.dma_start(norm.x[:, t % 2, :], rows_of(x2_d, n)).then_inc(norm.s_x[t % 2], 16)

                def store(b, h):
                    for d in range(DT):
                        c = b * KT + h * DT + d
                        sp.wait_ge(s_olo, made(c))
                        tok = slice(b * BANK, (b + 1) * BANK) if isinstance(b, int) else bass.ds(b * BANK, BANK)
                        sp.dma_start(o_d[0, h * DT + d, :, tok], raw(o_hi[:, d, :])).then_inc(s_st[d], 16)
                        sp.dma_start(o_d[1, h * DT + d, :, tok], raw(o_lo[:, d, :])).then_inc(s_st[d], 16)

                run(sp, {"f": load, "O": store})
                for d in range(DT):
                    sp.wait_ge(s_st[d], 32 * NBLK * XH)

            @block.gpsimd
            def _(pool):
                make_identity(room, pool, ident, s_ident)
                norm.start_pool(pool)

                def square_root(b, t):
                    norm.pool_rsqrt(pool, b * BT + BT + t, t % 2)

                run(pool, {"f": square_root})

            @block.scalar
            def _(act):
                norm.start_act(act)
                act.sem_inc(s_exp, RING)
                weight.high(act)

                def square(b, t):
                    norm.act_square(act, b * BT + BT + t, t % 2, b * (BT // 2) + BT // 2 + t // 2)

                def block_high(b, t):
                    for c in range(2):
                        norm.act_hi(act, b * BT + BT + t, c, h_hi[:, 4 * c:4 * c + 4, t * P:(t + 1) * P])

                def exps(b, u):
                    n = b * UNITS + u
                    act.wait_ge(s_minus, n + 1)
                    act.wait_ge(s_t, n - 1 + RING)
                    act.activation(probs[:, u % 2, :], sum_s[u % 2][:, 0:MEM], ACT.Exp, bias=minus[:, u % 4:u % 4 + 1],
                                   scale=XD ** -0.5, accum_out=total[:, u % 4:u % 4 + 1]).then_inc(s_exp, 1)

                def probs_high(b, u):
                    h, t = divmod(u, BT)
                    act.wait_ge(s_o, b * KT + h * DT - DT + 4)
                    act.wait_ge(s_t, b * UNITS + u + 1 + RING)
                    act.activation(t_hi[:, h % 2, :, t * P:(t + 1) * P],
                                   turned[:, 0:MEM].rearrange("p (k t) -> p k t", k=MT), ACT.Copy).then_inc(s_thi, 1)

                def queries_high(b, x):
                    if x % 2 == 1:
                        m = x // 2
                        act.wait_ge(s_q, b * KT + KT + m + 1)
                        act.activation(q_hi[:, m, :], sum_q[:, :], ACT.Copy).then_inc(s_qhi, 1)

                def out_high(b, h):
                    for d in range(DT):
                        act.wait_ge(s_st[d], b * (32 * XH) + 32 * h)
                        act.wait_ge(s_o, b * KT + h * DT + d + 1 + 4)
                        act.activation(o_hi[:, d, :], sum_o[d][:, :], ACT.Copy).then_inc(s_ohi, 1)

                run(act, {"f": square, "F": block_high, "S": exps, "T": probs_high, "Q": queries_high,
                          "O": out_high})

            @block.vector
            def _(dve):
                norm.start_dve(dve)
                dve.sem_inc(s_olo, RING)
                weight.low(dve)

                def scale(b, t):
                    norm.dve_scale(dve, b * BT + BT + t, t % 2)

                def block_low(b, t):
                    tok = slice(t * P, (t + 1) * P)
                    for c in range(2):
                        norm.dve_lo(dve, b * BT + BT + t, c, h_lo[:, 4 * c:4 * c + 4, tok],
                                    h_hi[:, 4 * c:4 * c + 4, tok])

                def maxima(b, u):
                    n = b * UNITS + u
                    dve.wait_ge(s_s, n + 1)
                    dve.reduce_max(top[:, u % 4:u % 4 + 1], sum_s[u % 2][:, 0:MEM], axis=AX.X).then_inc(s_max, 1)
                    dve.wait_ge(s_max, n + 1)
                    dve.tensor_scalar(minus[:, u % 4:u % 4 + 1], top[:, u % 4:u % 4 + 1], -(XD ** -0.5), None,
                                      ALU.mult).then_inc(s_minus, 1)
                    if u >= 1:
                        divide(b, u - 1)

                def divide(b, u):
                    n = b * UNITS + u
                    dve.wait_ge(s_exp, n + 1 + RING)
                    dve.reciprocal(share[:, u % 4:u % 4 + 1], total[:, u % 4:u % 4 + 1]).then_inc(s_share, 1)
                    dve.wait_ge(s_share, n + 1)
                    dve.tensor_scalar(probs[:, u % 2, :], probs[:, u % 2, :], share[:, u % 4:u % 4 + 1], None,
                                      ALU.mult).then_inc(s_p, 1)

                def probs_low(b, u):
                    h, t = divmod(u, BT)
                    if u == UNITS - 2:
                        divide(b, UNITS - 1)
                    dve.wait_ge(s_thi, b * UNITS + u + 1)
                    tok = slice(t * P, (t + 1) * P)
                    dve.tensor_tensor(t_lo[:, h % 2, :, tok], turned[:, 0:MEM].rearrange("p (k t) -> p k t", k=MT),
                                      raw(t_hi[:, h % 2, :, tok]), ALU.subtract).then_inc(s_tlo, 1)

                def queries_low(b, x):
                    if x % 2 == 1:
                        m = x // 2
                        dve.wait_ge(s_qhi, b * KT + KT + m + 1)
                        dve.tensor_tensor(q_lo[:, m, :], sum_q[:, :], raw(q_hi[:, m, :]),
                                          ALU.subtract).then_inc(s_qlo, 1)

                def out_low(b, h):
                    for d in range(DT):
                        dve.wait_ge(s_ohi, b * KT + h * DT + d + 1)
                        dve.tensor_tensor(o_lo[:, d, :], sum_o[d][:, :], raw(o_hi[:, d, :]),
                                          ALU.subtract).then_inc(s_olo, 1)

                run(dve, {"g": scale, "F": block_low, "S": maxima, "T": probs_low, "Q": queries_low,
                          "O": out_low})

            @block.tensor
            def _(pe):
                norm.start_pe(pe)
                pe.sem_inc(s_t, RING)
                pe.sem_inc(s_o, 4)
                pe.wait_ge(s_ident, 2)
                pe.wait_ge(weight.s_lo, KT)
                pe.wait_ge(s_kv, 64)

                def turn_block(b, t):
                    norm.pe_turn(pe, ident[:, :], b * BT + BT + t, t % 2)

                def queries(b, x):
                    m, part = divmod(x, 2)
                    if x == 0:
                        pe.wait_ge(norm.s_lo, (b * BT + BT + BT) * 2 + RING)
                    if part == 0:
                        pe.wait_ge(s_qlo, b * KT + KT + m)
                    for k in range(part * KT // 2, (part + 1) * KT // 2):
                        last = split3(pe, sum_q[:, :], weight.hi[:, k, m * P:(m + 1) * P],
                                      weight.lo[:, k, m * P:(m + 1) * P], h_hi[:, k, :], h_lo[:, k, :],
                                      k == 0, k == KT - 1)
                    if part == 1:
                        last.then_inc(s_q, 1)

                def score(b, u):
                    h, t = divmod(u, BT)
                    n = b * UNITS + u
                    if u % BT == 0:
                        pe.wait_ge(s_qlo, b * KT + (h + 1) * DT)
                    pe.wait_ge(s_exp, n - 1 + RING)
                    for d in range(DT):
                        m = h * DT + d
                        tok = slice(t * P, (t + 1) * P)
                        last = split3(pe, sum_s[u % 2][:, 0:MEM], q_hi[:, m, tok], q_lo[:, m, tok],
                                      k_p[0][:, m, :], k_p[1][:, m, :], d == 0, d == DT - 1)
                    last.then_inc(s_s, 1)

                def turn(b, u):
                    n = b * UNITS + u
                    pe.wait_ge(s_p, n + 1)
                    pe.wait_ge(s_tlo, n)
                    for k in range(MT):
                        last = pe.transpose(turned[:, k * P:(k + 1) * P], probs[:, u % 2, k * P:(k + 1) * P],
                                            ident[:, :])
                    last.then_inc(s_t, 1)

                def values(b, h):
                    pe.wait_ge(s_tlo, b * UNITS + (h + 1) * BT)
                    for d in range(DT):
                        c = b * KT + h * DT + d
                        pe.wait_ge(s_olo, c + 1 - DT + RING)
                        dims = slice((h * DT + d) * P, (h * DT + d + 1) * P)
                        for k in range(MT):
                            last = split3(pe, sum_o[d][:, :], v_p[0][:, k, dims], v_p[1][:, k, dims],
                                          t_hi[:, h % 2, k, :], t_lo[:, h % 2, k, :], k == 0, k == MT - 1)
                        last.then_inc(s_o, 1)

                run(pe, {"F": turn_block, "Q": queries, "S": score, "T": turn, "O": values})


def stage_cross_out(nc, o_d, w_co, x2_d, g_ffn, x3_d, h_d):
    with ExitStack() as ctx:
        room = Room(nc, ctx, "xout")
        out = room.sb("out", [P, 2, D])
        norm = Norm(room, x=out)
        weight = Resident(room, "w", w_co)
        ident = room.sb("ident", [P, P])
        o_p = [room.sb(f"o{part}", [P, 2, KT, P], F32R) for part in range(2)]
        res = room.sb("res", [P, 2, D])
        h_hi = room.sb("h_hi", [P, 2, KT, P], F32R)
        h_lo = room.sb("h_lo", [P, 2, KT, P], F32R)
        acc = [room.bank(f"acc{i}") for i in range(4)]
        s_ident = room.sem("s_ident")
        s_o = [room.sem(f"s_o{j}") for j in range(2)]
        s_acc = room.sem("s_acc")
        s_sum = room.sem("s_sum")
        s_stx = [room.sem(f"s_stx{j}") for j in range(2)]
        s_sth = [room.sem(f"s_sth{j}") for j in range(2)]
        PAIRS = NT // 2

        with nc.Block() as block:
            @block.sync
            def _(sp):
                def load(n, j):
                    for part in range(2):
                        tok = slice(n * P, (n + 1) * P) if isinstance(n, int) else bass.ds(n * P, P)
                        sp.dma_start(raw(o_p[part][:, j, :, :]),
                                     o_d[part, :, :, tok].rearrange("k p t -> p k t")).then_inc(s_o[j], 16)
                    sp.dma_start(res[:, j, :], rows_of(x2_d, n)).then_inc(s_o[j], 16)

                sp.dma_start(norm.gain[:, :], g_ffn.to_broadcast([P, D])).then_inc(norm.s_gain, 16)
                for j in range(2):
                    load(j, j)
                weight.load(sp)

                def pair(i, more):
                    for j in range(2):
                        n = i * 2 + j
                        tok = slice(n * P, (n + 1) * P) if isinstance(n, int) else bass.ds(n * P, P)
                        sp.wait_ge(s_sum, n * 2 + 2 + 4)
                        sp.dma_start(rows_of(x3_d, n), out[:, j, :]).then_inc(s_stx[j], 16)
                        if more:
                            load(n + 2, j)
                        sp.wait_ge(norm.s_lo, n * 2 + 2 + RING)
                        room.gate(sp)
                        sp.dma_start(h_d[0, :, :, tok].rearrange("k p t -> p k t"),
                                     raw(h_hi[:, j, :, :])).then_inc(s_sth[j], 16)
                        sp.dma_start(h_d[1, :, :, tok].rearrange("k p t -> p k t"),
                                     raw(h_lo[:, j, :, :])).then_inc(s_sth[j], 16)

                over_pairs(sp, PAIRS, pair)
                for j in range(2):
                    sp.wait_ge(s_stx[j], 16 * PAIRS)
                    sp.wait_ge(s_sth[j], 32 * PAIRS)

            @block.gpsimd
            def _(pool):
                make_identity(room, pool, ident, s_ident)
                norm.start_pool(pool)
                with pool.Fori(0, PAIRS) as i:
                    for j in range(2):
                        norm.pool_rsqrt(pool, i * 2 + j, j)

            @block.scalar
            def _(act):
                norm.start_act(act)
                weight.high(act)
                with act.Fori(0, PAIRS) as i:
                    for j in range(2):
                        n = i * 2 + j
                        act.wait_ge(s_sum, n * 2 + 2 + 4)
                        norm.act_square(act, n, j, None)
                        act.wait_ge(s_sth[j], 32 * i)
                        for b in range(2):
                            norm.act_hi(act, n, b, h_hi[:, j, 4 * b:4 * b + 4, :])

            @block.vector
            def _(dve):
                norm.start_dve(dve)
                dve.sem_inc(s_sum, 4)
                weight.low(dve)

                def total(i, j):
                    n = i * 2 + j
                    dve.wait_ge(s_o[j], i * 48 + 48)
                    dve.wait_ge(s_stx[j], 16 * i)
                    for b in range(2):
                        cols = slice(b * BANK, (b + 1) * BANK)
                        dve.wait_ge(s_acc, n * 2 + b + 1 + 4)
                        dve.tensor_tensor(out[:, j, cols], acc[j * 2 + b][:, :], res[:, j, cols],
                                          ALU.add).then_inc(s_sum, 1)

                def shape(n, j):
                    norm.dve_scale(dve, n, j)
                    for b in range(2):
                        norm.dve_lo(dve, n, b, h_lo[:, j, 4 * b:4 * b + 4, :], h_hi[:, j, 4 * b:4 * b + 4, :])

                with dve.Fori(0, PAIRS) as i:
                    for j in range(2):
                        total(i, j)
                        shape(i * 2 + j, j)

            @block.tensor
            def _(pe):
                norm.start_pe(pe)
                pe.sem_inc(s_acc, 4)
                pe.wait_ge(s_ident, 2)
                pe.wait_ge(weight.s_lo, KT)

                def multiply(i, j, between):
                    n = i * 2 + j
                    pe.wait_ge(s_o[j], i * 48 + 48)
                    for b in range(2):
                        cols = slice(b * BANK, (b + 1) * BANK)
                        pe.wait_ge(s_sum, n * 2 + b + 1)
                        for k in range(KT):
                            last = split3(pe, acc[j * 2 + b][:, :], o_p[0][:, j, k, :], o_p[1][:, j, k, :],
                                          weight.hi[:, k, cols], weight.lo[:, k, cols], k == 0, k == KT - 1)
                        last.then_inc(s_acc, 1)
                        if b == 0:
                            between()

                def turn(n, j):
                    norm.pe_turn(pe, ident[:, :], n, j)

                multiply(0, 0, lambda: None)
                multiply(0, 1, lambda: turn(0, 0))
                with pe.Fori(1, PAIRS) as i:
                    multiply(i, 0, lambda: turn(i * 2 - 1, 1))
                    multiply(i, 1, lambda: turn(i * 2, 0))
                turn(NT - 1, 1)


def stage_ffn(nc, h_d, x3_d, w_gate, w_up, w_down, g_final, out_d):
    with ExitStack() as ctx:
        room = Room(nc, ctx, "ffn")
        BLK = HALF // BANK
        DN = HT * 2
        h_p = [room.sb(f"h{part}", [P, KT, HALF], F32R) for part in range(2)]
        y = room.sb("y", [P, HT, D])
        kinds = ("gate", "up", "down")
        w_raw = {c: room.sb(f"{c}_raw", [P, D]) for c in kinds}
        w_hi = {c: room.sb(f"{c}_hi", [P, 2, D], F32R) for c in kinds}
        w_lo = {c: room.sb(f"{c}_lo", [P, 2, D], F32R) for c in kinds}
        silu = room.sb("silu", [P, BLK, BANK])
        a = room.sb("a", [P, BLK, BANK])
        a_hi = room.sb("a_hi", [P, 2, HALF], F32R)
        a_lo = room.sb("a_lo", [P, 2, HALF], F32R)
        gain = room.sb("gain", [P, D])
        ss = room.sb("ss", [P, HT])
        ms = room.sb("ms", [P, HT])
        rs = room.sb("rs", [P, HT])
        power = room.sb("power", [P, HT])
        sum_g = [room.bank(f"sum_g{b}") for b in range(BLK)]
        sum_u = [room.bank(f"sum_u{b}") for b in range(BLK)]
        sum_d = [room.bank(f"sum_d{b}") for b in range(4)]
        s_h = room.sem("s_h")
        s_y = room.sem("s_y")
        s_gain = room.sem("s_gain")
        s_w = {c: room.sem(f"s_{c}_in") for c in kinds}
        s_whi = {c: room.sem(f"s_{c}_hi") for c in kinds}
        s_wlo = {c: room.sem(f"s_{c}_lo") for c in kinds}
        s_g = room.sem("s_gate_sum")
        s_u = room.sem("s_up_sum")
        s_dn = room.sem("s_down_sum")
        s_silu = room.sem("s_silu")
        s_a = room.sem("s_a")
        s_ahi = room.sem("s_a_hi")
        s_alo = room.sem("s_a_lo")
        s_add = room.sem("s_added")
        s_ss = room.sem("s_ss")
        s_rs = room.sem("s_rs")
        s_fin = room.sem("s_fin")
        s_st = room.sem("s_st")
        source = {"gate": w_gate, "up": w_up, "down": w_down}

        with nc.Block() as block:
            @block.sync
            def _(sp):
                def load(c, F, f):
                    sp.wait_ge(s_wlo[c], F)
                    sp.dma_start(w_raw[c][:, :], source[c][bass.ds(f, 1), :, :].rearrange("a p c -> p (a c)")
                                 ).then_inc(s_w[c], 16)

                sp.dma_start(gain[:, :], g_final.to_broadcast([P, D])).then_inc(s_gain, 16)
                with sp.Fori(0, 2) as hf:
                    half = bass.ds(hf * HALF, HALF)
                    sp.wait_ge(s_u, hf * (FT * BLK) + 2)
                    for part in range(2):
                        sp.dma_start(raw(h_p[part][:, :, :]), h_d[part, :, :, half].rearrange("k p t -> p k t")
                                     ).then_inc(s_h, 16)
                    for c in ("gate", "up"):
                        load(c, hf * FT, hf * 0)
                    sp.wait_ge(s_st, hf * 16)
                    sp.dma_start(y[:, :, :], x3_d[half, :].rearrange("(t p) d -> p t d", p=P)).then_inc(s_y, 16)
                    load("down", hf * FT, hf * 0)
                    with sp.Fori(1, FT) as f:
                        for c in kinds:
                            load(c, hf * FT + f, f)

            @block.gpsimd
            def _(pool):
                pool.memset(power[:, :], -0.5).then_inc(s_rs, 1)

                def split(F, j):
                    for c in kinds:
                        pool.wait_ge(s_w[c], F * 16 + 16)
                        if c == "down":
                            pool.wait_ge(s_dn, F * DN + DN)
                        else:
                            pool.wait_ge(s_g if c == "gate" else s_u, F * BLK)
                        room.gate(pool)
                        pool.tensor_scalar(w_hi[c][:, j, :], w_raw[c][:, :], 1.0, 1.0,
                                           ALU.mult, ALU.mult).then_inc(s_whi[c], 1)
                        pool.wait_ge(s_whi[c], F + 1)
                        pool.tensor_tensor(w_lo[c][:, j, :], w_raw[c][:, :], raw(w_hi[c][:, j, :]),
                                           ALU.subtract).then_inc(s_wlo[c], 1)

                with pool.Fori(0, 2) as hf:
                    with pool.Fori(0, FT // 2) as i:
                        for j in range(2):
                            split(hf * FT + i * 2 + j, j)
                    pool.wait_ge(s_ss, hf * HT + HT)
                    room.gate(pool)
                    pool.tensor_scalar(ms[:, :], ss[:, :], 1.0 / D, EPS, ALU.mult, ALU.add).then_inc(s_rs, 1)
                    pool.wait_ge(s_rs, hf * 2 + 2)
                    pool.tensor_tensor(rs[:, :], ms[:, :], power[:, :], ALU.pow).then_inc(s_rs, 1)

            @block.scalar
            def _(act):
                act.sem_inc(s_silu, 2)

                def hidden(F, j):
                    for b in range(BLK):
                        act.wait_ge(s_g, F * BLK + b + 1 + 2)
                        act.wait_ge(s_a, F * BLK + b + 1)
                        act.activation(silu[:, b, :], sum_g[b][:, :], ACT.Silu).then_inc(s_silu, 1)
                        act.wait_ge(s_dn, F * DN + DN)
                        act.wait_ge(s_a, F * BLK + b + 1 + 2)
                        act.activation(a_hi[:, j, b * BANK:(b + 1) * BANK], a[:, b, :], ACT.Copy).then_inc(s_ahi, 1)

                with act.Fori(0, 2) as hf:
                    with act.Fori(0, FT // 2) as i:
                        for j in range(2):
                            hidden(hf * FT + i * 2 + j, j)
                    act.wait_ge(s_add, hf * (FT * DN) + FT * DN + DN)
                    for t in range(HT):
                        act.wait_ge(s_ss, hf * HT + t)
                        act.activation(silu[:, :, :].rearrange("p b c -> p (b c)"), y[:, t, :], ACT.Square,
                                       accum_out=ss[:, t:t + 1]).then_inc(s_ss, 1)
                    act.wait_ge(s_fin, hf + 1)
                    act.dma_start(out_d[bass.ds(hf * HALF, HALF), :].rearrange("(t p) d -> p t d", p=P),
                                  y[:, :, :]).then_inc(s_st, 16)
                act.wait_ge(s_st, 32)

            @block.vector
            def _(dve):
                dve.sem_inc(s_a, 2)
                dve.sem_inc(s_alo, 2)
                dve.sem_inc(s_add, DN)
                dve.wait_ge(s_gain, 16)

                def product(F, b):
                    dve.wait_ge(s_silu, F * BLK + b + 1 + 2)
                    dve.wait_ge(s_alo, F * BLK + b + 1)
                    dve.wait_ge(s_u, F * BLK + b + 1 + 2)
                    dve.tensor_tensor(a[:, b, :], sum_u[b][:, :], silu[:, b, :], ALU.mult).then_inc(s_a, 1)

                def low(F, j, b):
                    dve.wait_ge(s_ahi, F * BLK + b + 1)
                    cols = slice(b * BANK, (b + 1) * BANK)
                    dve.tensor_tensor(a_lo[:, j, cols], a[:, b, :], raw(a_hi[:, j, cols]),
                                      ALU.subtract).then_inc(s_alo, 1)

                def add(F, q):
                    for z in range(DN // 4):
                        d = q * (DN // 4) + z
                        t, n = divmod(d, 2)
                        dve.wait_ge(s_dn, F * DN + d + 1 + 2 * DN)
                        dve.wait_ge(s_add, F * DN + d + 1)
                        cols = slice(n * BANK, (n + 1) * BANK)
                        dve.tensor_tensor(y[:, t, cols], sum_d[d % 4][:, :], y[:, t, cols],
                                          ALU.add).then_inc(s_add, 1)

                def both(F, j):
                    add(F - 1, 0)
                    product(F, 0)
                    add(F - 1, 1)
                    low(F, j, 0)
                    add(F - 1, 2)
                    product(F, 1)
                    add(F - 1, 3)
                    low(F, j, 1)

                with dve.Fori(0, 2) as hf:
                    for b in range(BLK):
                        product(hf * FT, b)
                        low(hf * FT, 0, b)
                    dve.wait_ge(s_y, hf * 16 + 16)
                    room.gate(dve)
                    with dve.Fori(0, FT // 2 - 1) as i:
                        for j in range(2):
                            both(hf * FT + i * 2 + j + 1, (j + 1) % 2)
                    both(hf * FT + (FT - 1), 1)
                    for q in range(4):
                        add(hf * FT + (FT - 1), q)
                    dve.wait_ge(s_rs, hf * 2 + 3)
                    for t in range(HT):
                        last = dve.scalar_tensor_tensor(y[:, t, :], y[:, t, :], rs[:, t:t + 1], gain[:, :],
                                                        ALU.mult, ALU.mult)
                    last.then_inc(s_fin, 1)

            @block.tensor
            def _(pe):
                pe.sem_inc(s_g, 2)
                pe.sem_inc(s_u, 2)
                pe.sem_inc(s_dn, 2 * DN)

                def down(F, j, q):
                    for z in range(DN // 4):
                        d = q * (DN // 4) + z
                        t, n = divmod(d, 2)
                        pe.wait_ge(s_add, F * DN + d + 1 - 4 + DN)
                        tok, cols = slice(t * P, (t + 1) * P), slice(n * BANK, (n + 1) * BANK)
                        split3(pe, sum_d[d % 4][:, :], a_hi[:, j, tok], a_lo[:, j, tok],
                               w_hi["down"][:, j, cols], w_lo["down"][:, j, cols], True, True).then_inc(s_dn, 1)

                def make(F, j, between):
                    for b in range(BLK):
                        for c, bank, s_sum, s_read in (("gate", sum_g, s_g, s_silu), ("up", sum_u, s_u, s_a)):
                            pe.wait_ge(s_wlo[c], F + 1)
                            pe.wait_ge(s_read, F * BLK + b + 1)
                            cols = slice(b * BANK, (b + 1) * BANK)
                            for k in range(KT):
                                wk = slice(k * P, (k + 1) * P)
                                last = split3(pe, bank[b][:, :], w_hi[c][:, j, wk], w_lo[c][:, j, wk],
                                              h_p[0][:, k, cols], h_p[1][:, k, cols], k == 0, k == KT - 1)
                            last.then_inc(s_sum, 1)
                            between(b * 2 + (c == "up"))

                def both(F, j):
                    def quarter(q):
                        if q == 0:
                            pe.wait_ge(s_alo, F * BLK + 2)
                            pe.wait_ge(s_wlo["down"], F)
                        down(F - 1, (j + 1) % 2, q)
                    make(F, j, quarter)

                with pe.Fori(0, 2) as hf:
                    pe.wait_ge(s_h, hf * 32 + 32)
                    make(hf * FT, 0, lambda q: None)
                    with pe.Fori(0, FT // 2 - 1) as i:
                        for j in range(2):
                            both(hf * FT + i * 2 + j + 1, (j + 1) % 2)
                    both(hf * FT + (FT - 1), 1)
                    pe.wait_ge(s_alo, hf * (FT * BLK) + FT * BLK + 2)
                    pe.wait_ge(s_wlo["down"], hf * FT + FT)
                    for q in range(4):
                        down(hf * FT + (FT - 1), 1, q)


_INPUTS = ["x", "mem", "positions", "freq", "g_mix", "w_qk", "b_qk", "w_v", "b_v", "sinks", "rel_rev", "g_grp",
           "w_out", "g_cross", "g_mem", "w_cq", "w_xk", "w_xv", "w_co", "g_ffn", "w_gate", "w_up", "w_down",
           "g_final"]


def build(nc, a, out):
    def scratch(name, shape):
        return nc.dram_tensor(name, shape, F32, kind="Internal").ap()

    cos_d, sin_d = scratch("cos_d", [P, SEQ]), scratch("sin_d", [P, SEQ])
    ext_d = scratch("ext_d", [P, 8 * EXT])
    bias_d = scratch("bias_d", [8, P, B_WIN * P])
    kx_d, vx_d = scratch("kx_d", [2, P, KT * MEM]), scratch("vx_d", [2, P, MT * D])
    qk_d = scratch("qk_d", [2, N_QK, P, SEQ])
    v_d = scratch("v_d", [2, SEQ, 2 * V_GROUP])
    mix_d, x2_d, x3_d = (scratch(n, [SEQ, D]) for n in ("mix_d", "x2_d", "x3_d"))
    o_d, h_d = (scratch(n, [2, KT, P, SEQ]) for n in ("o_d", "h_d"))

    stage_tables(nc, a["positions"], a["freq"], a["rel_rev"], cos_d, sin_d, ext_d, bias_d)
    stage_memory(nc, a["mem"], a["g_mem"], a["w_xk"], a["w_xv"], kx_d, vx_d)
    stage_qkv(nc, a["x"], a["g_mix"], a["w_qk"], a["b_qk"], a["w_v"], a["b_v"], cos_d, sin_d, qk_d, v_d)
    stage_attention(nc, "a", qk_d, v_d, mix_d, None, a["sinks"])
    stage_attention(nc, "b", qk_d, v_d, mix_d, bias_d, None)
    stage_mix(nc, mix_d, a["g_grp"], a["x"], a["w_out"], x2_d)
    stage_cross(nc, x2_d, a["g_cross"], a["w_cq"], kx_d, vx_d, o_d)
    stage_cross_out(nc, o_d, a["w_co"], x2_d, a["g_ffn"], x3_d, h_d)
    stage_ffn(nc, h_d, x3_d, a["w_gate"], a["w_up"], a["w_down"], a["g_final"], out)


def by_tile(w, width):
    rows, cols = w.shape
    w = w.reshape(rows // P, P, cols // width, width).transpose(2, 1, 0, 3)
    return w.reshape(cols // width, P, rows // P * width)


def kernel(**inputs):
    import concourse.bacc as bacc
    from concourse.bass_utils import run_bass_kernel_spmd

    a = {name: np.asarray(v) for name, v in inputs.items()}
    w_in, b_in = a["w_in"][0], a["b_in"][0]
    ends = np.cumsum([A_Q, A_KV, A_KV, B_W, B_W, B_W])
    qa, ka, va, qb, kb, vb = (slice(e - w, e) for e, w in zip(ends, (A_Q, A_KV, A_KV, B_W, B_W, B_W)))

    def joined(w):
        k = w[..., ka]
        return np.concatenate([w[..., qa], k[..., :HD], k[..., :HD], k[..., HD:], k[..., HD:],
                               w[..., qb], w[..., kb]], axis=-1)

    step = np.arange(HD // 2, dtype=np.float32) * np.float32(2.0 / HD)
    inverse = (np.float32(1.0) / (THETA ** step.astype(np.float64)).astype(np.float32)).astype(np.float32)
    freq = np.stack([np.tile(inverse, 4), np.tile(np.repeat(np.float32([-1.0, 1.0]), HD // 2), 2)], axis=1)

    arrays = {
        "x": a["x"][0], "mem": a["mem"][0], "positions": a["positions"], "freq": freq,
        "g_mix": a["g_mix"], "w_qk": by_tile(joined(w_in), P), "b_qk": joined(b_in).reshape(N_QK, P).T,
        "w_v": by_tile(np.concatenate([w_in[:, va], w_in[:, vb]], axis=1), V_GROUP),
        "b_v": np.concatenate([b_in[va], b_in[vb]])[None],
        "sinks": a["sinks"], "rel_rev": a["rel_bias"][0][:, ::-1],
        "g_grp": np.concatenate([a["g_grp_a"], a["g_grp_b"]], axis=1),
        "w_out": a["w_out"][0].reshape(KT, P, D), "g_cross": a["g_cross"], "g_mem": a["g_mem"],
        "w_cq": a["w_cq"][0].reshape(KT, P, D), "w_xk": by_tile(a["w_ckv"][0][:, :D], P),
        "w_xv": by_tile(a["w_ckv"][0][:, D:], 256), "w_co": a["w_co"][0].reshape(KT, P, D),
        "g_ffn": a["g_ffn"], "w_gate": by_tile(a["w_gate"][0], P), "w_up": by_tile(a["w_up"][0], P),
        "w_down": a["w_down"][0].reshape(FT, P, D), "g_final": a["g_final"][None],
    }
    arrays = {name: np.ascontiguousarray(arrays[name]) for name in _INPUTS}

    nc = bacc.Bacc("TRN2", target_bir_lowering=False, num_devices=1)
    aps = {n: nc.dram_tensor(f"in_{n}", v.shape, mybir.dt.from_np(v.dtype), kind="ExternalInput").ap()
           for n, v in arrays.items()}
    out = nc.dram_tensor("out", (SEQ, D), F32, kind="ExternalOutput").ap()
    build(nc, aps, out)
    r = run_bass_kernel_spmd(nc, [{f"in_{n}": v for n, v in arrays.items()}], core_ids=[0])
    return r.results[0]["out"].reshape(1, SEQ, D)
```

```python
import math
from contextlib import ExitStack, nullcontext

import numpy as np

import concourse.bass as bass
from concourse import mybir

F32 = mybir.dt.float32
F32R = mybir.dt.float32r
I32 = mybir.dt.int32
ALU = mybir.AluOpType
ACT = mybir.ActivationFunctionType
AX = mybir.AxisListType

P = 128
D = 1024
SEQ = 2048
HALF = SEQ // 2
KT = D // P
NT = SEQ // P
HT = HALF // P
BANK = 512
HD = 64
CHUNK = 64
EPS = 1e-6
THETA = 10000.0
NEG = -1e30
A_Q, A_KV, B_W = 512, 128, 512
N_PAIR = 4
A_WIN, B_WIN = 2, 5
REL_CLIP = 256
N_REL = 2 * REL_CLIP + 1
MEM = 256
MT = MEM // P
XH, XD = 4, 256
FF = 2816
FT = FF // P
V_GROUP = 320
N_QK = 14
N_QK_A = 6
EXT = 768


def split3(pe, out, l_hi, l_lo, r_hi, r_lo, first, last):
    pe.matmul(out, l_hi, r_hi, start=first, stop=False)
    pe.matmul(out, l_hi, r_lo, start=False, stop=False)
    return pe.matmul(out, l_lo, r_hi, start=False, stop=last)


def raw(ap):
    return ap.bitcast(F32)


class Room:

    def __init__(self, nc, ctx, stage):
        self.nc, self.ctx, self.stage, self.sems = nc, ctx, stage, []
        ctx.callback(self.close)
        self.s_gate = self.sem("s_gate")

    def gate(self, engine):
        engine.sem_inc(self.s_gate, 1)

    def sb(self, name, shape, dt=F32):
        return self.ctx.enter_context(self.nc.sbuf_tensor(f"{self.stage}_{name}", shape, dt))

    def bank(self, name, n=1):
        return self.ctx.enter_context(self.nc.psum_tensor(f"{self.stage}_{name}", [P, n * BANK], F32))

    def sem(self, name):
        semaphore = self.nc.alloc_semaphore(f"{self.stage}_{name}")
        self.sems.append(semaphore)
        return semaphore

    def close(self):
        self.nc.clear_and_free_semaphores(self.sems)
        self.nc.all_engine_barrier()


RING = 2


def made(n):
    return n + 1 + RING


def free(n):
    return n + 1


class Norm:

    def __init__(self, room, groups=1, x=None):
        self.room = room
        self.groups = groups
        self.x = room.sb("x", [P, 2, D]) if x is None else x
        self.xn = room.sb("xn", [P, 2, D])
        self.gain = room.sb("gain", [P, D])
        self.ss = room.sb("ss", [P, 2, groups])
        self.ms = room.sb("ms", [P, 2, groups])
        self.rs = room.sb("rs", [P, 2, groups])
        self.power = room.sb("power", [P, groups])
        self.turned = [room.bank(f"turned{b}") for b in range(2)]
        self.s_gain = room.sem("s_gain")
        self.s_x = [room.sem(f"s_x{j}") for j in range(2)]
        self.s_ss = room.sem("s_ss")
        self.s_ms = room.sem("s_ms")
        self.s_rs = room.sem("s_rs")
        self.s_xn = room.sem("s_xn")
        self.s_turned = room.sem("s_turned")
        self.s_hi = room.sem("s_turned_hi")
        self.s_lo = room.sem("s_turned_lo")
        self.s_power = room.sem("s_power")

    def start_act(self, act):
        act.sem_inc(self.s_ss, RING)

    def start_pool(self, pool):
        pool.memset(self.power[:, :], -0.5).then_inc(self.s_power, 1)
        pool.sem_inc(self.s_rs, RING)
        pool.wait_ge(self.s_power, 1)

    def start_dve(self, dve):
        dve.sem_inc(self.s_xn, RING)
        dve.sem_inc(self.s_lo, RING)
        dve.wait_ge(self.s_gain, 16)

    def start_pe(self, pe):
        pe.sem_inc(self.s_turned, 2 * RING)

    def act_square(self, act, n, j, use):
        x = self.x[:, j, :]
        if use is not None:
            act.wait_ge(self.s_x[j], 16 * use + 16)
        act.wait_ge(self.s_rs, free(n))
        act.wait_ge(self.s_turned, 2 * n + 2)
        w = D // self.groups
        for g in range(self.groups):
            last = act.activation(self.xn[:, j, g * w:(g + 1) * w], x[:, g * w:(g + 1) * w],
                                  ACT.Square, accum_out=self.ss[:, j, g:g + 1])
        last.then_inc(self.s_ss, 1)

    def pool_rsqrt(self, pool, n, j):
        pool.wait_ge(self.s_ss, made(n))
        pool.wait_ge(self.s_xn, free(n))
        self.room.gate(pool)
        pool.tensor_scalar(self.ms[:, j, :], self.ss[:, j, :], float(self.groups) / D, EPS,
                           ALU.mult, ALU.add).then_inc(self.s_ms, 1)
        pool.wait_ge(self.s_ms, n + 1)
        pool.tensor_tensor(self.rs[:, j, :], self.ms[:, j, :], self.power[:, :],
                           ALU.pow).then_inc(self.s_rs, 1)

    def dve_scale(self, dve, n, j):
        x = self.x[:, j, :]
        dve.wait_ge(self.s_rs, made(n))
        dve.wait_ge(self.s_turned, 2 * n + 2)
        w = D // self.groups
        for g in range(self.groups):
            cols = slice(g * w, (g + 1) * w)
            last = dve.scalar_tensor_tensor(self.xn[:, j, cols], x[:, cols], self.rs[:, j, g:g + 1],
                                            self.gain[:, cols], ALU.mult, ALU.mult)
        last.then_inc(self.s_xn, 1)

    def pe_turn(self, pe, ident, n, j):
        pe.wait_ge(self.s_xn, made(n))
        for b in range(2):
            pe.wait_ge(self.s_lo, 2 * n + b + 1)
            for q in range(4):
                k = 4 * b + q
                last = pe.transpose(self.turned[b][:, q * P:(q + 1) * P],
                                    self.xn[:, j, k * P:(k + 1) * P], ident)
            last.then_inc(self.s_turned, 1)

    def act_hi(self, act, n, b, out):
        act.wait_ge(self.s_turned, 2 * n + b + 1 + 2 * RING)
        act.activation(out, self.turned[b][:, :].rearrange("p (k t) -> p k t", k=4),
                       ACT.Copy).then_inc(self.s_hi, 1)

    def act_whole(self, act, n, b, out):
        act.wait_ge(self.s_turned, 2 * n + b + 1 + 2 * RING)
        act.activation(out, self.turned[b][:, :].rearrange("p (k t) -> p k t", k=4),
                       ACT.Copy).then_inc(self.s_lo, 1)

    def dve_lo(self, dve, n, b, out, hi):
        dve.wait_ge(self.s_hi, 2 * n + b + 1)
        dve.tensor_tensor(out, self.turned[b][:, :].rearrange("p (k t) -> p k t", k=4), raw(hi),
                          ALU.subtract).then_inc(self.s_lo, 1)


def make_identity(room, pool, ident, s_ident):
    pool.memset(ident[:, :], 0.0).then_inc(s_ident, 1)
    pool.wait_ge(s_ident, 1)
    pool.affine_select(out=ident[:, :], in_=ident[:, :], compare_op=ALU.not_equal, fill=1.0, base=0,
                       pattern=[[-1, P]], channel_multiplier=1).then_inc(s_ident, 1)


def stage_tables(nc, positions, freq, rel_rev, cos_d, sin_d, ext_d, bias_d):
    with ExitStack() as ctx:
        room = Room(nc, ctx, "tables")
        pos_i = room.sb("pos_i", [P, SEQ], I32)
        ang = room.sb("ang", [P, SEQ])
        turns = room.sb("turns", [P, SEQ])
        turns_i = room.sb("turns_i", [P, SEQ], I32)
        wrap = room.sb("wrap", [P, SEQ])
        sin = room.sb("sin", [P, SEQ])
        cos = room.sb("cos", [P, SEQ])
        fr = room.sb("fr", [P, 2])
        rel = room.sb("rel", [P, 8, N_REL])
        ext = room.sb("ext", [P, 8, EXT])
        band = room.sb("band", [P, 8, B_WIN * P])
        s_mask = room.sem("s_mask")
        s_in = room.sem("s_in")
        s_rel = room.sem("s_rel")
        s_v = room.sem("s_v")
        s_sin = room.sem("s_sin")
        s_act = room.sem("s_act")
        s_ext = room.sem("s_ext")
        s_out = room.sem("s_out")
        two_pi = 2.0 * math.pi
        c1 = 6.28125
        c2 = float(np.float32(np.round((two_pi - c1) * 2.0 ** 21) / 2.0 ** 21))
        c3 = two_pi - c1 - c2
        pi_in = 3.1415925

        with nc.Block() as block:
            @block.sync
            def _(sp):
                sp.dma_start(pos_i[:, :], positions.to_broadcast([P, SEQ])).then_inc(s_in, 16)
                sp.dma_start(fr[:, :], freq).then_inc(s_in, 16)
                sp.dma_start(rel[:, :, :].rearrange("p h r -> p (h r)"),
                             rel_rev.rearrange("(a h) r -> a (h r)", a=1).to_broadcast([P, 8 * N_REL])
                             ).then_inc(s_rel, 16)
                sp.wait_ge(s_sin, 1)
                sp.dma_start(sin_d, sin[:, :]).then_inc(s_out, 16)
                sp.wait_ge(s_act, 2)
                sp.dma_start(cos_d, cos[:, :]).then_inc(s_out, 16)
                sp.wait_ge(s_ext, 2)
                sp.dma_start(ext_d, ext[:, :, :].rearrange("p h n -> p (h n)")).then_inc(s_out, 16)
                sp.wait_ge(s_out, 48)
                win = B_WIN * P
                rows = bass.AP(ext_d.tensor, P - 1, [[8 * EXT - 1, P], [EXT, 8], [1, win]])
                sp.dma_start(band[:, :, :], rows).then_inc(s_in, 16)
                sp.wait_ge(s_mask, 2)
                sp.dma_start(bias_d.rearrange("h p n -> p h n"), band[:, :, :]).then_inc(s_out, 16)
                sp.wait_ge(s_out, 64)

            @block.vector
            def _(dve):
                done = [0]

                def then(instruction):
                    done[0] += 1
                    instruction.then_inc(s_v, 1)
                    dve.wait_ge(s_v, done[0])

                dve.wait_ge(s_in, 32)
                then(dve.tensor_copy(ang[:, :], pos_i[:, :]))
                then(dve.tensor_scalar(ang[:, :], ang[:, :], fr[:, 0:1], None, ALU.mult))
                then(dve.tensor_scalar(turns[:, :], ang[:, :], 1.0 / two_pi, None, ALU.mult))
                then(dve.tensor_copy(turns_i[:, :], turns[:, :]))
                then(dve.tensor_copy(turns[:, :], turns_i[:, :]))
                for c in (c1, c2, c3):
                    then(dve.scalar_tensor_tensor(ang[:, :], turns[:, :], -c, ang[:, :], ALU.mult, ALU.add))
                for _ in range(1):
                    then(dve.tensor_scalar(wrap[:, :], ang[:, :], math.pi, -two_pi, ALU.is_gt, ALU.mult))
                    then(dve.tensor_tensor(ang[:, :], ang[:, :], wrap[:, :], ALU.add))
                    then(dve.tensor_scalar(wrap[:, :], ang[:, :], -math.pi, two_pi, ALU.is_lt, ALU.mult))
                    then(dve.tensor_tensor(ang[:, :], ang[:, :], wrap[:, :], ALU.add))
                then(dve.tensor_scalar(turns[:, :], ang[:, :], math.pi / 2, None, ALU.add))
                then(dve.tensor_scalar(wrap[:, :], turns[:, :], math.pi, -two_pi, ALU.is_gt, ALU.mult))
                then(dve.tensor_tensor(turns[:, :], turns[:, :], wrap[:, :], ALU.add))
                then(dve.tensor_scalar(turns[:, :], turns[:, :], pi_in, -pi_in, ALU.min, ALU.max))
                then(dve.tensor_scalar(ang[:, :], ang[:, :], pi_in, -pi_in, ALU.min, ALU.max))
                dve.wait_ge(s_act, 1)
                dve.tensor_scalar(sin[:, :], sin[:, :], fr[:, 1:2], None, ALU.mult).then_inc(s_sin, 1)

            @block.gpsimd
            def _(pool):
                flat = (B_WIN * P - 1) - REL_CLIP
                pool.wait_ge(s_rel, 16)
                pool.tensor_scalar(ext[:, :, 0:flat], rel[:, :, 0:1].to_broadcast([P, 8, flat]), 8.0, 1.0,
                                   ALU.mult, ALU.mult).then_inc(s_ext, 1)
                pool.tensor_scalar(ext[:, :, flat:EXT], rel[:, :, 0:EXT - flat], 8.0, 1.0,
                                   ALU.mult, ALU.mult).then_inc(s_ext, 1)
                pool.wait_ge(s_in, 48)
                pool.memset(band[0:CHUNK, :, B_WIN * P - CHUNK:], NEG).then_inc(s_mask, 1)
                pool.memset(band[CHUNK:P, :, 0:CHUNK], NEG).then_inc(s_mask, 1)

            n_dve = 5 + 3 + 4 + 5

            @block.scalar
            def _(act):
                act.wait_ge(s_v, n_dve)
                act.activation(sin[:, :], ang[:, :], ACT.Sin).then_inc(s_act, 1)
                act.activation(cos[:, :], turns[:, :], ACT.Sin).then_inc(s_act, 1)


def stage_memory(nc, mem, g_mem, w_k, w_v, kx_d, vx_d):
    with ExitStack() as ctx:
        room = Room(nc, ctx, "mem")
        norm = Norm(room)
        ident = room.sb("ident", [P, P])
        m_hi = room.sb("m_hi", [P, KT, MEM], F32R)
        m_lo = room.sb("m_lo", [P, KT, MEM], F32R)
        N_K, N_V, VW = KT, 4, 256
        w_raw = room.sb("w_raw", [P, 3, KT * VW])
        w_hi = room.sb("w_hi", [P, 2, KT * VW], F32R)
        w_lo = room.sb("w_lo", [P, 2, KT * VW], F32R)
        k_out = room.sb("k_out", [P, 2, N_K, MEM], F32R)
        v_out = room.sb("v_out", [P, 2, MT, D], F32R)
        acc = [room.bank(f"acc{i}") for i in range(2)]
        s_ident = room.sem("s_ident")
        s_w = [room.sem(f"s_w{i}") for i in range(3)]
        s_hi = room.sem("s_w_hi")
        s_lo = room.sem("s_w_lo")
        s_acc = room.sem("s_acc")
        s_ohi = room.sem("s_out_hi")
        s_olo = room.sem("s_out_lo")
        s_out = room.sem("s_out")
        items = [("k", m, KT * P) for m in range(N_K)] + [("v", c, KT * VW) for c in range(N_V)]
        accs = [(kind, m, t) for kind, m, _ in items for t in (range(1) if kind == "k" else range(MT))]

        acc_end = [sum(1 if kind == "k" else MT for kind, _, _ in items[:n + 1])
                   for n in range(len(items))]

        def target(kind, m, t, part):
            if kind == "k":
                return k_out[:, part, m, :]
            return v_out[:, part, t, m * VW:(m + 1) * VW]

        with nc.Block() as block:
            @block.sync
            def _(sp):
                for j in range(MT):
                    sp.dma_start(norm.x[:, j, :], mem[j * P:(j + 1) * P, :]).then_inc(norm.s_x[j], 16)
                sp.dma_start(norm.gain[:, :], g_mem.to_broadcast([P, D])).then_inc(norm.s_gain, 16)
                for n, (kind, m, w) in enumerate(items):
                    if n >= 3:
                        sp.wait_ge(s_lo, n - 2)
                    src = w_k[m] if kind == "k" else w_v[m]
                    sp.dma_start(w_raw[:, n % 3, 0:w], src).then_inc(s_w[n % 3], 16)
                sp.wait_ge(s_olo, len(accs))
                for part in range(2):
                    sp.dma_start(kx_d[part], raw(k_out[:, part, :, :].rearrange("p m t -> p (m t)"))).then_inc(s_out, 16)
                    sp.dma_start(vx_d[part], raw(v_out[:, part, :, :].rearrange("p t d -> p (t d)"))).then_inc(s_out, 16)
                sp.wait_ge(s_out, 64)

            @block.gpsimd
            def _(pool):
                make_identity(room, pool, ident, s_ident)
                norm.start_pool(pool)
                for n in range(MT):
                    norm.pool_rsqrt(pool, n, n)
                for n, (kind, m, w) in enumerate(items):
                    pool.wait_ge(s_hi, n + 1)
                    pool.tensor_tensor(w_lo[:, n % 2, 0:w], w_raw[:, n % 3, 0:w], raw(w_hi[:, n % 2, 0:w]),
                                       ALU.subtract).then_inc(s_lo, 1)

            @block.scalar
            def _(act):
                norm.start_act(act)
                for n in range(MT):
                    norm.act_square(act, n, n, 0)
                for n in range(MT):
                    for b in range(2):
                        norm.act_hi(act, n, b, m_hi[:, 4 * b:4 * b + 4, n * P:(n + 1) * P])
                for a, (kind, m, t) in enumerate(accs):
                    act.wait_ge(s_acc, a + 1)
                    act.activation(target(kind, m, t, 0), acc[a % 2][:, 0:VW], ACT.Copy).then_inc(s_ohi, 1)

            @block.vector
            def _(dve):
                norm.start_dve(dve)
                for n in range(MT):
                    norm.dve_scale(dve, n, n)
                for n in range(MT):
                    for b in range(2):
                        norm.dve_lo(dve, n, b, m_lo[:, 4 * b:4 * b + 4, n * P:(n + 1) * P],
                                    m_hi[:, 4 * b:4 * b + 4, n * P:(n + 1) * P])

                def w_high(n):
                    kind, m, w = items[n]
                    dve.wait_ge(s_w[n % 3], 16 * (n // 3) + 16)
                    if n >= 2:
                        dve.wait_ge(s_acc, acc_end[n - 2])
                    dve.tensor_copy(w_hi[:, n % 2, 0:w], w_raw[:, n % 3, 0:w]).then_inc(s_hi, 1)

                w_high(0)
                w_high(1)
                a = 0
                for n, (kind, m, w) in enumerate(items):
                    for t in (range(1) if kind == "k" else range(MT)):
                        dve.wait_ge(s_ohi, a + 1)
                        dve.tensor_tensor(target(kind, m, t, 1), acc[a % 2][:, 0:VW],
                                          raw(target(kind, m, t, 0)), ALU.subtract).then_inc(s_olo, 1)
                        a += 1
                    if n + 2 < len(items):
                        w_high(n + 2)

            @block.tensor
            def _(pe):
                norm.start_pe(pe)
                pe.wait_ge(s_ident, 2)
                for n in range(MT):
                    norm.pe_turn(pe, ident[:, :], n, n)
                pe.wait_ge(norm.s_lo, 2 * MT + RING)
                a = 0
                for n, (kind, m, w) in enumerate(items):
                    pe.wait_ge(s_lo, n + 1)
                    hi = w_hi[:, n % 2, 0:w].rearrange("p (k c) -> p k c", k=KT)
                    lo = w_lo[:, n % 2, 0:w].rearrange("p (k c) -> p k c", k=KT)
                    for t in (range(1) if kind == "k" else range(MT)):
                        if a >= 2:
                            pe.wait_ge(s_olo, a - 1)
                        for k in range(KT):
                            if kind == "k":
                                last = split3(pe, acc[a % 2][:, 0:MEM], hi[:, k, :], lo[:, k, :],
                                              m_hi[:, k, :], m_lo[:, k, :], k == 0, k == KT - 1)
                            else:
                                tok = slice(t * P, (t + 1) * P)
                                last = split3(pe, acc[a % 2][:, 0:VW], m_hi[:, k, tok], m_lo[:, k, tok],
                                              hi[:, k, :], lo[:, k, :], k == 0, k == KT - 1)
                        last.then_inc(s_acc, 1)
                        a += 1


def stage_qkv(nc, x, g_mix, w_qk, b_qk, w_v, b_v, cos_d, sin_d, qk_d, v_d):
    with ExitStack() as ctx:
        room = Room(nc, ctx, "qkv")
        norm = Norm(room)
        ident = room.sb("ident", [P, P])
        h_hi = room.sb("h_hi", [P, KT, HALF], F32R)
        h_lo = room.sb("h_lo", [P, KT, HALF], F32R)
        W_COLS = KT * V_GROUP
        w_raw = room.sb("w_raw", [P, 2, W_COLS])
        w_hi = room.sb("w_hi", [P, 2, W_COLS], F32R)
        w_lo = room.sb("w_lo", [P, 2, W_COLS], F32R)
        bias = room.sb("bias", [P, N_QK])
        bias_v = room.sb("bias_v", [P, 2 * V_GROUP])
        cos = room.sb("cos", [P, SEQ])
        sin = room.sb("sin", [P, SEQ])
        y = room.sb("y", [P, 2, HALF])
        swapped = room.sb("swapped", [P, HALF])
        cos_part = room.sb("cos_part", [P, HALF])
        o_hi = room.sb("o_hi", [P, 2, HALF], F32R)
        o_lo = room.sb("o_lo", [P, 2, HALF], F32R)
        values = room.sb("values", [P, 2, V_GROUP])
        acc = [room.bank(f"acc{i}") for i in range(4)]
        s_ident = room.sem("s_ident")
        s_const = room.sem("s_const")
        s_w = [room.sem(f"s_w{j}") for j in range(2)]
        s_whi = room.sem("s_w_hi")
        s_wlo = room.sem("s_w_lo")
        s_acc = room.sem("s_acc")
        s_read = room.sem("s_acc_read")
        s_swap = room.sem("s_swapped")
        s_cos = room.sem("s_products")
        s_y = room.sem("s_y")
        s_ohi = room.sem("s_out_hi")
        s_olo = room.sem("s_out_lo")
        s_st = [room.sem(f"s_stored{j}") for j in range(2)]
        s_vst = [room.sem(f"s_values_stored{j}") for j in range(2)]

        BLK = HALF // BANK
        ITEMS = N_QK + 2
        USES = N_QK * BLK + 2 * HT
        OUTS = N_QK
        EARLY = 16

        def blocks():
            return [(0, N_QK_A // 2, True), (N_QK_A // 2, (N_QK - N_QK_A) // 2, False)]

        with nc.Block() as block:
            @block.sync
            def _(sp):
                def load_x(hf, i, j):
                    n = hf * HT + i * 2 + j
                    sp.wait_ge(norm.s_xn, free(n))
                    sp.dma_start(norm.x[:, j, :], x[bass.ds(n * P, P), :]).then_inc(norm.s_x[j], 16)

                def load_w(hf, i, j):
                    m = i * 2 + j
                    sp.wait_ge(s_wlo, free(hf * ITEMS + m))
                    sp.dma_start(w_raw[:, j, 0:KT * P],
                                 w_qk[bass.ds(m, 1), :, :].rearrange("a p c -> p (a c)")).then_inc(s_w[j], 16)

                sp.dma_start(norm.gain[:, :], g_mix.to_broadcast([P, D])).then_inc(norm.s_gain, 16)
                sp.dma_start(bias[:, :], b_qk).then_inc(s_const, 16)
                sp.dma_start(bias_v[:, :], b_v.to_broadcast([P, 2 * V_GROUP])).then_inc(s_const, 16)
                sp.dma_start(cos[:, :], cos_d).then_inc(s_const, 16)
                sp.dma_start(sin[:, :], sin_d).then_inc(s_const, 16)
                with sp.Fori(0, 2) as hf:
                    with sp.Fori(0, HT // 2) as i:
                        for j in range(2):
                            load_x(hf, i, j)
                    with sp.Fori(0, N_QK // 2) as i:
                        for j in range(2):
                            load_w(hf, i, j)
                    for j in range(2):
                        sp.wait_ge(s_wlo, free(hf * ITEMS + N_QK + j))
                        sp.dma_start(w_raw[:, j, :], w_v[j]).then_inc(s_w[j], 16)

            @block.gpsimd
            def _(pool):
                make_identity(room, pool, ident, s_ident)
                norm.start_pool(pool)
                pool.sem_inc(s_wlo, RING)

                def split(n, j, use, used, w):
                    pool.wait_ge(s_w[j], 16 * use + 16)
                    pool.wait_ge(s_acc, used)
                    room.gate(pool)
                    pool.tensor_scalar(w_hi[:, j, 0:w], w_raw[:, j, 0:w], 1.0, 1.0,
                                       ALU.mult, ALU.mult).then_inc(s_whi, 1)
                    pool.wait_ge(s_whi, n + 1)
                    pool.tensor_tensor(w_lo[:, j, 0:w], w_raw[:, j, 0:w], raw(w_hi[:, j, 0:w]),
                                       ALU.subtract).then_inc(s_wlo, 1)

                with pool.Fori(0, 2) as hf:
                    with pool.Fori(0, HT // 2) as i:
                        for j in range(2):
                            norm.pool_rsqrt(pool, hf * HT + i * 2 + j, j)
                    for j in range(2):
                        split(hf * ITEMS + j, j, hf * (ITEMS // 2), hf * USES + EARLY - HT * (1 - j), KT * P)
                    with pool.Fori(1, N_QK // 2) as i:
                        for j in range(2):
                            split(hf * ITEMS + i * 2 + j, j, hf * (ITEMS // 2) + i,
                                  hf * USES + (i * 2 + j - 1) * BLK + EARLY, KT * P)
                    for j in range(2):
                        split(hf * ITEMS + N_QK + j, j, hf * (ITEMS // 2) + N_QK // 2,
                              hf * USES + (N_QK + j - 1) * BLK + EARLY, W_COLS)

            @block.scalar
            def _(act):
                norm.start_act(act)
                for j in range(2):
                    act.sem_inc(s_st[j], 32)

                def high(j, use, w, s_there, there):
                    act.wait_ge(s_st[j], 32 * use + 32)
                    act.wait_ge(s_there, there)
                    act.activation(o_hi[:, j, 0:w], y[:, j, 0:w], ACT.Copy).then_inc(s_ohi, 1)

                def store(o, j, hi_at, lo_at, w):
                    act.wait_ge(s_ohi, o + 1)
                    act.dma_start(hi_at, raw(o_hi[:, j, 0:w])).then_inc(s_st[j], 16)
                    act.wait_ge(s_olo, made(o))
                    act.dma_start(lo_at, raw(o_lo[:, j, 0:w])).then_inc(s_st[j], 16)

                def qk_at(part, m, hf):
                    return qk_d[part, bass.ds(m, 1), :, bass.ds(hf * HALF, HALF)].rearrange("a p t -> p (a t)")

                with act.Fori(0, 2) as hf:
                    with act.Fori(0, HT // 2) as i:
                        for j in range(2):
                            norm.act_square(act, hf * HT + i * 2 + j, j, hf * (HT // 2) + i)
                        for j in range(2):
                            for b in range(2):
                                act.wait_ge(norm.s_turned, 2 * (hf * HT + i * 2 + j) + b + 1 + 2 * RING)
                                room.gate(act)
                                tok = bass.ds(i * (2 * P) + j * P, P)
                                act.activation(h_hi[:, 4 * b:4 * b + 4, tok],
                                               norm.turned[b][:, :].rearrange("p (k t) -> p k t", k=4),
                                               ACT.Copy).then_inc(norm.s_hi, 1)
                    for first, pairs, rotated in blocks():
                        with act.Fori(first, first + pairs) as i:
                            for j in range(2):
                                m = i * 2 + j
                                o = hf * OUTS + m
                                biased = hf * USES + m * BLK + BLK + 4
                                if rotated:
                                    act.wait_ge(s_read, biased)
                                    act.wait_ge(s_y, hf * N_QK_A + m + 1)
                                    for head in (0, HD):
                                        for a, b in ((0, HD // 2), (HD // 2, 0)):
                                            act.dma_start(swapped[head + a:head + a + HD // 2, :],
                                                          y[head + b:head + b + HD // 2, j, :]).then_inc(s_swap, 16)
                                if rotated:
                                    high(j, hf * (OUTS // 2) + i, HALF, s_y, hf * N_QK_A + m + 2)
                                else:
                                    high(j, hf * (OUTS // 2) + i, HALF, s_read, biased)
                                store(o, j, qk_at(0, m, hf), qk_at(1, m, hf), HALF)
                    for g in range(2):
                        with act.Fori(0, HT // 2) as i:
                            for j in range(2):
                                act.wait_ge(s_read, hf * USES + N_QK * BLK + g * HT + i * 2 + j + 1 + 4)
                                rows = bass.ds(hf * HALF + i * (2 * P) + j * P, P)
                                act.dma_start(v_d[rows, g * V_GROUP:(g + 1) * V_GROUP],
                                              values[:, j, :]).then_inc(s_vst[j], 16)
                for j in range(2):
                    act.wait_ge(s_st[j], 32 * OUTS + 32)
                    act.wait_ge(s_vst[j], 16 * 2 * HT + 16)

            @block.vector
            def _(dve):
                norm.start_dve(dve)
                dve.sem_inc(s_read, 4)
                dve.sem_inc(s_olo, RING)
                dve.sem_inc(s_y, 1)
                for j in range(2):
                    dve.sem_inc(s_vst[j], 16)
                dve.wait_ge(s_const, 64)

                def low(o, j, w):
                    dve.wait_ge(s_ohi, o + 1)
                    dve.tensor_tensor(o_lo[:, j, 0:w], y[:, j, 0:w], raw(o_hi[:, j, 0:w]),
                                      ALU.subtract).then_inc(s_olo, 1)

                with dve.Fori(0, 2) as hf:
                    with dve.Fori(0, HT // 2) as i:
                        for j in range(2):
                            norm.dve_scale(dve, hf * HT + i * 2 + j, j)
                        for j in range(2):
                            tok = bass.ds(i * (2 * P) + j * P, P)
                            for b in range(2):
                                norm.dve_lo(dve, hf * HT + i * 2 + j, b, h_lo[:, 4 * b:4 * b + 4, tok],
                                            h_hi[:, 4 * b:4 * b + 4, tok])
                    for first, pairs, rotated in blocks():
                        with dve.Fori(first, first + pairs) as i:
                            for j in range(2):
                                m = i * 2 + j
                                o = hf * OUTS + m
                                dve.wait_ge(s_olo, free(o))
                                for b in range(BLK):
                                    dve.wait_ge(s_acc, hf * USES + m * BLK + b + 1 + EARLY)
                                    last = dve.tensor_scalar(y[:, j, b * BANK:(b + 1) * BANK],
                                                             acc[j * BLK + b][:, :], bias[:, bass.ds(m, 1)],
                                                             None, ALU.add)
                                    last.then_inc(s_read, 1)
                                here = slice(0, HALF)
                                dve.wait_ge(s_read, hf * USES + m * BLK + BLK + 4)
                                if rotated:
                                    r = hf * N_QK_A + m
                                    table = bass.ds(hf * HALF, HALF)
                                    dve.wait_ge(s_y, r + 1)
                                    dve.tensor_tensor(cos_part[:, :], y[:, j, here], cos[:, table],
                                                      ALU.mult).then_inc(s_cos, 1)
                                    dve.wait_ge(s_swap, 64 * r + 64)
                                    dve.tensor_tensor(swapped[:, :], swapped[:, :], sin[:, table],
                                                      ALU.mult).then_inc(s_cos, 1)
                                    dve.wait_ge(s_cos, 2 * r + 2)
                                    dve.tensor_tensor(y[:, j, here], cos_part[:, :], swapped[:, :],
                                                      ALU.add).then_inc(s_y, 1)
                                low(o, j, HALF)
                    for g in range(2):
                        with dve.Fori(0, HT // 4) as i:
                            for q in range(4):
                                tt = i * 4 + q
                                a = hf * USES + N_QK * BLK + g * HT + tt
                                dve.wait_ge(s_vst[q % 2], hf * (16 * HT) + g * (8 * HT) + i * 32 + 16 * (q // 2) + 16)
                                dve.wait_ge(s_acc, a + 1 + EARLY)
                                dve.tensor_tensor(values[:, q % 2, :], acc[q][:, 0:V_GROUP],
                                                  bias_v[:, g * V_GROUP:(g + 1) * V_GROUP],
                                                  ALU.add).then_inc(s_read, 1)

            @block.tensor
            def _(pe):
                norm.start_pe(pe)
                pe.sem_inc(s_acc, EARLY)
                pe.wait_ge(s_ident, 2)
                with pe.Fori(0, 2) as hf:
                    with pe.Fori(0, HT // 2) as i:
                        for j in range(2):
                            norm.pe_turn(pe, ident[:, :], hf * HT + i * 2 + j, j)
                    pe.wait_ge(norm.s_lo, hf * (2 * HT) + 2 * HT + RING)
                    room.gate(pe)
                    with pe.Fori(0, N_QK // 2) as i:
                        for j in range(2):
                            m = i * 2 + j
                            pe.wait_ge(s_wlo, made(hf * ITEMS + m))
                            for b in range(BLK):
                                a = hf * USES + m * BLK + b
                                pe.wait_ge(s_read, a + 1)
                                cols = slice(b * BANK, (b + 1) * BANK)
                                for k in range(KT):
                                    wk = slice(k * P, (k + 1) * P)
                                    last = split3(pe, acc[j * BLK + b][:, :], w_hi[:, j, wk], w_lo[:, j, wk],
                                                  h_hi[:, k, cols], h_lo[:, k, cols], k == 0, k == KT - 1)
                                last.then_inc(s_acc, 1)
                    for g in range(2):
                        pe.wait_ge(s_wlo, made(hf * ITEMS + N_QK + g))
                        for tt in range(HT):
                            a = hf * USES + N_QK * BLK + g * HT + tt
                            pe.wait_ge(s_read, a + 1)
                            tok = slice(tt * P, (tt + 1) * P)
                            for k in range(KT):
                                wk = slice(k * V_GROUP, (k + 1) * V_GROUP)
                                last = split3(pe, acc[tt % 4][:, 0:V_GROUP], h_hi[:, k, tok], h_lo[:, k, tok],
                                              w_hi[:, g, wk], w_lo[:, g, wk], k == 0, k == KT - 1)
                            last.then_inc(s_acc, 1)


def stage_attention(nc, group, qk_d, v_d, mix_d, bias_d, sinks8):
    is_a = group == "a"
    win = A_WIN if is_a else B_WIN
    bodies, pairs = (1, N_PAIR) if is_a else (2, 2)
    heads = 2 if is_a else 1
    q0, k0 = (0, 4) if is_a else (N_QK_A, N_QK_A + 4)
    kheads = 1 if is_a else 2
    vw = kheads * HD
    v0 = 0 if is_a else A_KV
    skip = CHUNK if is_a else 0

    units = [(pp, i, h) for pp in range(pairs) for h in range(0, 2, heads) for i in range(NT)]
    NB = len(units)
    per_pair = NB // pairs
    assert NB % 4 == 0

    def tiles(i):
        return min(i + 1, win)

    def blocks(i, piece):
        w = tiles(i)
        if is_a:
            return [(piece, y) for y in range(w)]
        half = (w + 1) // 2
        return [(0, y) for y in (range(0, half) if piece == 0 else range(half, w))]

    counts = [[0], [0]]
    for _, i, _ in units:
        for piece in range(2):
            counts[piece].append(counts[piece][-1] + (1 if blocks(i, piece) else 0))

    def pieces_before(g, u, piece):
        c = counts[piece]
        return g * c[NB] + (c[u] if u >= 0 else c[NB + u] - c[NB])

    with ExitStack() as ctx:
        room = Room(nc, ctx, f"att_{group}")
        ident = room.sb("ident", [P, P])
        q_t = room.sb("q", [P, 2, 2, SEQ], F32R)
        k_t = [room.sb(f"k{part}", [P, 2, kheads, SEQ], F32R) for part in range(2)]
        v_t = room.sb("v", [P, 2, NT, vw])
        SW = heads * win * P
        bias = room.sb("bias", [P, 2, win * P] if is_a else [P, 2, 2, win * P])
        sink = room.sb("sink", [P, 8])
        scores = room.sb("scores", [P, 2, SW])
        probs = room.sb("probs", [P, 4, SW])
        turned_sb = room.sb("turned_sb", [P, 2, SW])
        top = room.sb("top", [P, 4, heads])
        minus = room.sb("minus", [P, 4, heads])
        total = room.sb("total", [P, 4, heads])
        below = room.sb("below", [P, 4, heads])
        sink_exp = room.sb("sink_exp", [P, 4, heads])
        whole = room.sb("whole", [P, 4, heads])
        share = room.sb("share", [P, 4, heads])
        out = room.sb("out", [P, 2, NT, P])
        sum_s = [room.bank(f"sum_s{j}", 2) for j in range(2)]
        turned = [room.bank(f"turned{j}") for j in range(2)]
        sum_o = [room.bank(f"sum_o{j}") for j in range(2)]
        s_ident = room.sem("s_ident")
        s_const = room.sem("s_const")
        s_ld = [room.sem(f"s_ld{j}") for j in range(2)]
        s_bias = [room.sem(f"s_bias{j}") for j in range(2)]
        s_s = room.sem("s_scores")
        s_max = room.sem("s_max")
        s_minus = room.sem("s_minus")
        s_exp = room.sem("s_exp")
        s_sink = room.sem("s_sink")
        s_t = [room.sem(f"s_turned{p}") for p in range(2)]
        s_copied = [room.sem(f"s_copied{p}") for p in range(2)]
        s_o = room.sem("s_o")
        s_den = room.sem("s_den")
        s_out = room.sem("s_out")
        s_st = [room.sem(f"s_st{j}") for j in range(2)]
        s_zero = room.sem("s_zero")

        def body(engine):
            return engine.Fori(0, bodies) if bodies > 1 else nullcontext(0)

        EARLY = per_pair + 4

        def copy(engine, instruction, g, u, piece):
            pp, i, h = units[u]
            if not blocks(i, piece):
                return
            engine.wait_ge(s_o, g * NB + u - 1 + EARLY)
            engine.wait_ge(s_t[piece], pieces_before(g, u + 1, piece) + EARLY)
            x, y = blocks(i, piece)[0]
            cols = slice((x * win + y) * P, (x * win + y + len(blocks(i, piece))) * P)
            instruction(turned_sb[:, u % 2, cols],
                        turned[piece][:, 0:len(blocks(i, piece)) * P]).then_inc(s_copied[piece], 1)

        with nc.Block() as block:
            @block.sync
            def _(sp):
                if is_a:
                    sp.dma_start(sink[:, :], sinks8.to_broadcast([P, 8])).then_inc(s_const, 16)
                with body(sp) as g:
                    for pp in range(pairs):
                        j = pp % 2
                        sp.wait_ge(s_o, g * NB + (pp - 1) * per_pair + EARLY)
                        for part in range(2):
                            half = slice(part * HD, (part + 1) * HD)
                            at = q0 + pp if is_a else bass.ds(q0 + g * pairs + pp, 1)
                            if is_a:
                                src = qk_d[part, at, :, :].rearrange("(h r) t -> r h t", h=2)
                            else:
                                src = qk_d[part, at, :, :].rearrange("a (h r) t -> r (a h) t", h=2)
                            sp.dma_start(raw(q_t[half, j, :, :]), src).then_inc(s_ld[j], 16)
                        for part in range(2):
                            for copy_at in (slice(0, HD), slice(HD, P)):
                                if is_a and pp % 2 == 0:
                                    kv = pp // 2
                                    sp.dma_start(raw(k_t[part][copy_at, kv, 0, :]),
                                                 qk_d[part, k0 + kv, 0:HD, :]).then_inc(s_ld[j], 16)
                                if not is_a:
                                    at = bass.ds(k0 + g * pairs + pp, 1)
                                    sp.dma_start(raw(k_t[part][copy_at, j, :, :]),
                                                 qk_d[part, at, :, :].rearrange("a (h r) t -> r (a h) t", h=2)
                                                 ).then_inc(s_ld[j], 16)
                        if is_a and pp % 2 == 0:
                            kv = pp // 2
                            sp.dma_start(v_t[:, kv, :, :], v_d[:, kv * HD:(kv + 1) * HD].rearrange(
                                "(i p) c -> p i c", p=P)).then_inc(s_ld[j], 16)
                        if not is_a:
                            cols = bass.ds(g * (pairs * P) + (v0 + pp * P), P)
                            sp.dma_start(v_t[:, j, :, :],
                                         v_d[:, cols].rearrange("(i p) c -> p i c", p=P)).then_inc(s_ld[j], 16)
                            sp.wait_ge(s_max, g * NB + (pp - 1) * per_pair + EARLY)
                            heads_at = bass.ds(g * (2 * pairs) + 2 * pp, 2)
                            sp.dma_start(bias[:, j, :, :], bias_d[heads_at, :, :].rearrange("h p n -> p h n")
                                         ).then_inc(s_bias[j], 16)

            def loaded(g, pp):
                return (7 * 16, 2 * 16, 14 * 16, 4 * 16)[pp] if is_a else g * (7 * 16) + 7 * 16

            @block.gpsimd
            def _(pool):
                make_identity(room, pool, ident, s_ident)
                pool.memset(probs[:, :, :], 0.0).then_inc(s_zero, 1)
                if is_a:
                    pool.memset(bias[:, :, :], 0.0).then_inc(s_zero, 1)
                    pool.wait_ge(s_zero, 2)
                    pool.memset(bias[0:CHUNK, 0, 3 * CHUNK:4 * CHUNK], NEG).then_inc(s_zero, 1)
                    pool.memset(bias[CHUNK:P, 0, CHUNK:2 * CHUNK], NEG).then_inc(s_zero, 1)

            @block.scalar
            def _(act):
                act.sem_inc(s_exp, RING)
                act.sem_inc(s_copied[0], EARLY)
                act.wait_ge(s_zero, 4 if is_a else 1)

                def exps(g, u):
                    pp, i, h = units[u]
                    act.wait_ge(s_minus, g * NB + u + 1)
                    for piece in range(2):
                        act.wait_ge(s_t[piece], pieces_before(g, u - 3, piece) + EARLY)
                    w = tiles(i) * P - (skip if tiles(i) == win else 0)
                    for x in range(heads):
                        last = act.activation(probs[:, u % 4, (x + 1) * win * P - w:(x + 1) * win * P],
                                              scores[:, u % 2, (x + 1) * win * P - w:(x + 1) * win * P], ACT.Exp,
                                              bias=minus[:, u % 4, x:x + 1], scale=0.125,
                                              accum_out=total[:, u % 4, x:x + 1])
                    if is_a:
                        last = act.activation(sink_exp[:, u % 4, :], below[:, u % 4, :], ACT.Exp, scale=0.125)
                    last.then_inc(s_exp, 1)

                def copied(out, in_):
                    return act.activation(out, in_, ACT.Copy)

                def store(g, pp):
                    act.wait_ge(s_out, g * NB + (pp + 1) * per_pair + 4)
                    cols0 = (0 if is_a else A_Q) + pp * P
                    cols = slice(cols0, cols0 + P) if is_a else bass.ds(g * (pairs * P) + cols0, P)
                    act.dma_start(mix_d[:, cols].rearrange("(i p) c -> p i c", p=P),
                                  out[:, pp % 2, :, :]).then_inc(s_st[pp % 2], 16)

                with body(act) as g:
                    for step in range(NB + 2):
                        if step >= 2:
                            copy(act, copied, g, step - 2, 0)
                        if step < NB:
                            exps(g, step)
                        if step >= per_pair and step % per_pair == 6:
                            store(g, step // per_pair - 1)
                    store(g, pairs - 1)
                for j in range(2):
                    act.wait_ge(s_st[j], 16 * bodies * pairs // 2 + 16)

            @block.vector
            def _(dve):
                dve.sem_inc(s_max, EARLY)
                dve.sem_inc(s_copied[1], EARLY)
                dve.sem_inc(s_out, 4)
                for j in range(2):
                    dve.sem_inc(s_st[j], 16)
                if is_a:
                    dve.wait_ge(s_const, 16)
                    dve.tensor_scalar(sink[:, :], sink[:, :], 8.0, None, ALU.mult).then_inc(s_sink, 1)
                    dve.wait_ge(s_sink, 1)
                    dve.wait_ge(s_zero, 4)

                def maxima(g, u):
                    pp, i, h = units[u]
                    n = g * NB + u
                    w = tiles(i) * P - (skip if tiles(i) == win else 0)
                    if not is_a and u % per_pair == 0:
                        dve.wait_ge(s_bias[pp % 2], g * 16 + 16)
                    dve.wait_ge(s_exp, n + 1)
                    dve.wait_ge(s_s, n + 1)
                    room.gate(dve)
                    for x in range(heads):
                        head = pp * 2 + h + x
                        window = slice((x + 1) * win * P - w, (x + 1) * win * P)
                        to = scores[:, u % 2, window]
                        if is_a:
                            add = bias[:, 0, win * P - w:win * P]
                            start = sink[:, head:head + 1]
                        else:
                            add = bias[:, pp % 2, h, win * P - w:win * P]
                            start = -3e38
                        if w <= BANK:
                            end = tiles(i) * P
                            from_ = sum_s[u % 2][:, x * BANK + end - w:x * BANK + end]
                        else:
                            from_ = sum_s[u % 2][:, :].rearrange("p (b c) -> p b c", b=2)[:, :, 0:w // 2]
                            to = to.rearrange("p (b c) -> p b c", b=2)
                            add = add.rearrange("p (b c) -> p b c", b=2)
                        last = dve.tensor_tensor_reduce(
                            out=to, in0=from_, in1=add, scale=1.0, scalar=start, op0=ALU.add, op1=ALU.max,
                            accum_out=top[:, u % 4, x:x + 1])
                    last.then_inc(s_max, 1)
                    dve.wait_ge(s_max, n + 1 + EARLY)
                    last = dve.tensor_scalar(minus[:, u % 4, :], top[:, u % 4, :], -0.125, None, ALU.mult)
                    if is_a:
                        first = pp * 2
                        last = dve.tensor_tensor(below[:, u % 4, :], sink[:, first:first + 2], top[:, u % 4, :],
                                                 ALU.subtract)
                    last.then_inc(s_minus, 1)

                def divide(g, u):
                    pp, i, h = units[u]
                    n = g * NB + u
                    j = pp % 2
                    denominator = total[:, u % 4, :]
                    steps = 2 if is_a else 1
                    if is_a:
                        dve.tensor_tensor(whole[:, u % 4, :], total[:, u % 4, :], sink_exp[:, u % 4, :],
                                          ALU.add).then_inc(s_den, 1)
                        dve.wait_ge(s_den, n * steps + 1)
                        denominator = whole[:, u % 4, :]
                    dve.reciprocal(share[:, u % 4, :], denominator).then_inc(s_den, 1)
                    dve.wait_ge(s_o, n + 1 + EARLY)
                    if u % per_pair == 0:
                        dve.wait_ge(s_st[j], (16 * (pp // 2) if is_a else g * 16) + 16)
                    dve.wait_ge(s_den, n * steps + steps)
                    at = out[:, j, i, h * HD:(h + heads) * HD].rearrange("p (h c) -> p h c", h=heads)
                    dve.tensor_tensor(at, sum_o[u % 2][:, 0:heads * HD].rearrange("p (h c) -> p h c", h=heads),
                                      share[:, u % 4, :].unsqueeze(2).to_broadcast([P, heads, HD]),
                                      ALU.mult).then_inc(s_out, 1)

                with body(dve) as g:
                    for step in range(NB + 3):
                        if step < NB:
                            maxima(g, step)
                        if 2 <= step < NB + 2:
                            copy(dve, dve.tensor_copy, g, step - 2, 1)
                        if step >= 3:
                            divide(g, step - 3)

            @block.tensor
            def _(pe):
                for piece in range(2):
                    pe.sem_inc(s_t[piece], EARLY)
                pe.sem_inc(s_o, EARLY)
                pe.wait_ge(s_ident, 2)

                def score(g, u):
                    pp, i, h = units[u]
                    n = g * NB + u
                    if u % per_pair == 0:
                        pe.wait_ge(s_ld[pp % 2], loaded(g, pp))
                    pe.wait_ge(s_max, n - 1 + EARLY)
                    w = tiles(i) * P
                    key0 = (i + 1) * P - w
                    parts = [(0, w, 0)] if w <= BANK else [(0, w // 2, 0), (w // 2, w, BANK)]
                    for x in range(heads):
                        qs = q_t[:, pp % 2, h + x, i * P:(i + 1) * P]
                        ks = (pp // 2, 0) if is_a else (pp % 2, h)
                        for a, b, bank in parts:
                            for part in range(2):
                                last = pe.matmul(sum_s[u % 2][:, x * BANK + bank:x * BANK + bank + b - a], qs,
                                                 k_t[part][:, ks[0], ks[1], key0 + a:key0 + b],
                                                 start=part == 0, stop=part == 1)
                    last.then_inc(s_s, 1)

                def turn(g, u):
                    pp, i, h = units[u]
                    n = g * NB + u
                    pe.wait_ge(s_exp, n + 1 + RING)
                    for piece in range(2):
                        if not blocks(i, piece):
                            continue
                        pe.wait_ge(s_copied[piece], pieces_before(g, u, piece) + EARLY)
                        for z, (x, y) in enumerate(blocks(i, piece)):
                            at = (x + 1) * win - tiles(i) + y
                            last = pe.transpose(turned[piece][:, z * P:(z + 1) * P],
                                                probs[:, u % 4, at * P:(at + 1) * P], ident[:, :])
                        last.then_inc(s_t[piece], 1)

                def values(g, u):
                    pp, i, h = units[u]
                    n = g * NB + u
                    for piece in range(2):
                        if blocks(i, piece):
                            pe.wait_ge(s_copied[piece], pieces_before(g, u + 1, piece) + EARLY)
                    pe.wait_ge(s_out, n + 3)
                    w = tiles(i)
                    vs = (pp // 2) if is_a else pp % 2
                    for x in range(heads):
                        cols = slice(0, HD) if is_a else slice(h * HD, (h + 1) * HD)
                        for y in range(w):
                            kt = i + 1 - w + y
                            at = slice((x * win + y) * P, (x * win + y + 1) * P)
                            last = pe.matmul(sum_o[u % 2][:, x * HD:(x + 1) * HD], turned_sb[:, u % 2, at],
                                             v_t[:, vs, kt, cols], start=y == 0, stop=y == w - 1)
                    last.then_inc(s_o, 1)

                with body(pe) as g:
                    for step in range(NB + 3):
                        if step < NB:
                            score(g, step)
                        if 2 <= step < NB + 2:
                            turn(g, step - 2)
                        if step >= 3:
                            values(g, step - 3)


class Resident:

    def __init__(self, room, name, weight, stage=None):
        self.weight = weight
        self.stage = room.sb(f"{name}_raw", [P, 2, D]) if stage is None else stage
        self.hi = room.sb(f"{name}_hi", [P, KT, D], F32R)
        self.lo = room.sb(f"{name}_lo", [P, KT, D], F32R)
        self.s_in = [room.sem(f"s_{name}_in{j}") for j in range(2)]
        self.s_hi = room.sem(f"s_{name}_hi")
        self.s_lo = room.sem(f"s_{name}_lo")

    def load(self, sp):
        for k in range(KT):
            if k >= 2:
                sp.wait_ge(self.s_lo, k - 1)
            sp.dma_start(self.stage[:, k % 2, :], self.weight[k]).then_inc(self.s_in[k % 2], 16)

    def high(self, act):
        for k in range(KT):
            act.wait_ge(self.s_in[k % 2], 16 * (k // 2) + 16)
            act.activation(self.hi[:, k, :], self.stage[:, k % 2, :], ACT.Copy).then_inc(self.s_hi, 1)

    def low(self, dve):
        for k in range(KT):
            dve.wait_ge(self.s_hi, k + 1)
            dve.tensor_tensor(self.lo[:, k, :], self.stage[:, k % 2, :], raw(self.hi[:, k, :]),
                              ALU.subtract).then_inc(self.s_lo, 1)


def over_pairs(engine, pairs, body):
    with engine.Fori(0, pairs - 1) as i:
        body(i, True)
    body(pairs - 1, False)


def rows_of(tensor, n):
    return tensor[n * P:(n + 1) * P, :] if isinstance(n, int) else tensor[bass.ds(n * P, P), :]


def stage_mix(nc, mix_d, gain, x, w_out, x2_d):
    with ExitStack() as ctx:
        room = Room(nc, ctx, "mix")
        norm = Norm(room, groups=2)
        weight = Resident(room, "w", w_out)
        ident = room.sb("ident", [P, P])
        m_hi = room.sb("m_hi", [P, 2, KT, P], F32R)
        m_lo = room.sb("m_lo", [P, 2, KT, P], F32R)
        res = room.sb("res", [P, 2, D])
        out = room.sb("out", [P, 2, D])
        acc = [room.bank(f"acc{i}") for i in range(4)]
        s_ident = room.sem("s_ident")
        s_res = [room.sem(f"s_res{j}") for j in range(2)]
        s_acc = room.sem("s_acc")
        s_sum = room.sem("s_sum")
        s_st = [room.sem(f"s_st{j}") for j in range(2)]
        PAIRS = NT // 2

        with nc.Block() as block:
            @block.sync
            def _(sp):
                sp.dma_start(norm.gain[:, :], gain.to_broadcast([P, D])).then_inc(norm.s_gain, 16)
                for j in range(2):
                    sp.dma_start(norm.x[:, j, :], rows_of(mix_d, j)).then_inc(norm.s_x[j], 16)
                    sp.dma_start(res[:, j, :], rows_of(x, j)).then_inc(s_res[j], 16)
                weight.load(sp)

                def pair(i, more):
                    for j in range(2):
                        n = i * 2 + j
                        if more:
                            sp.wait_ge(norm.s_xn, made(n))
                            sp.dma_start(norm.x[:, j, :], rows_of(mix_d, n + 2)).then_inc(norm.s_x[j], 16)
                        sp.wait_ge(s_sum, n * 2 + 2 + 4)
                        sp.dma_start(rows_of(x2_d, n), out[:, j, :]).then_inc(s_st[j], 16)
                        if more:
                            sp.dma_start(res[:, j, :], rows_of(x, n + 2)).then_inc(s_res[j], 16)

                over_pairs(sp, PAIRS, pair)
                for j in range(2):
                    sp.wait_ge(s_st[j], 16 * PAIRS + 16)

            @block.gpsimd
            def _(pool):
                make_identity(room, pool, ident, s_ident)
                norm.start_pool(pool)
                with pool.Fori(0, PAIRS) as i:
                    for j in range(2):
                        norm.pool_rsqrt(pool, i * 2 + j, j)

            @block.scalar
            def _(act):
                norm.start_act(act)

                def shape(n, j, use):
                    norm.act_square(act, n, j, use)
                    act.wait_ge(s_acc, n * 2 - 2 + 4)
                    for b in range(2):
                        norm.act_hi(act, n, b, m_hi[:, j, 4 * b:4 * b + 4, :])

                shape(0, 0, 0)
                weight.high(act)

                def pair(i, more):
                    shape(i * 2 + 1, 1, i)
                    if more:
                        shape(i * 2 + 2, 0, i + 1)

                over_pairs(act, PAIRS, pair)

            @block.vector
            def _(dve):
                norm.start_dve(dve)
                dve.sem_inc(s_sum, 4)
                for j in range(2):
                    dve.sem_inc(s_st[j], 16)

                def shape(n, j):
                    norm.dve_scale(dve, n, j)
                    for b in range(2):
                        norm.dve_lo(dve, n, b, m_lo[:, j, 4 * b:4 * b + 4, :], m_hi[:, j, 4 * b:4 * b + 4, :])

                shape(0, 0)
                weight.low(dve)

                def pair(i, more):
                    for j in range(2):
                        n = i * 2 + j
                        if more or j == 0:
                            shape(n + 1, (j + 1) % 2)
                        dve.wait_ge(s_res[j], 16 * i + 16)
                        dve.wait_ge(s_st[j], 16 * i + 16)
                        for b in range(2):
                            cols = slice(b * BANK, (b + 1) * BANK)
                            dve.wait_ge(s_acc, n * 2 + b + 1 + 4)
                            dve.tensor_tensor(out[:, j, cols], acc[j * 2 + b][:, :], res[:, j, cols],
                                              ALU.add).then_inc(s_sum, 1)

                over_pairs(dve, PAIRS, pair)

            @block.tensor
            def _(pe):
                norm.start_pe(pe)
                pe.sem_inc(s_acc, 4)
                pe.wait_ge(s_ident, 2)
                norm.pe_turn(pe, ident[:, :], 0, 0)
                pe.wait_ge(weight.s_lo, KT)

                def pair(i, more):
                    for j in range(2):
                        n = i * 2 + j
                        pe.wait_ge(norm.s_lo, n * 2 + 2 + RING)
                        for b in range(2):
                            cols = slice(b * BANK, (b + 1) * BANK)
                            pe.wait_ge(s_sum, n * 2 + b + 1)
                            for k in range(KT):
                                last = split3(pe, acc[j * 2 + b][:, :], m_hi[:, j, k, :], m_lo[:, j, k, :],
                                              weight.hi[:, k, cols], weight.lo[:, k, cols],
                                              k == 0, k == KT - 1)
                            last.then_inc(s_acc, 1)
                            if b == 0 and (more or j == 0):
                                norm.pe_turn(pe, ident[:, :], n + 1, (j + 1) % 2)

                over_pairs(pe, PAIRS, pair)


def stage_cross(nc, x2_d, g_cross, w_cq, kx_d, vx_d, o_d):
    with ExitStack() as ctx:
        room = Room(nc, ctx, "cross")
        norm = Norm(room)
        BT = BANK // P
        NBLK = SEQ // BANK
        UNITS = XH * BT
        DT = XD // P
        ident = room.sb("ident", [P, P])
        h_hi = room.sb("h_hi", [P, KT, BANK], F32R)
        h_lo = room.sb("h_lo", [P, KT, BANK], F32R)
        q_hi = room.sb("q_hi", [P, KT, BANK], F32R)
        q_lo = room.sb("q_lo", [P, KT, BANK], F32R)
        k_p = [room.sb(f"k{part}", [P, KT, MEM], F32R) for part in range(2)]
        v_p = [room.sb(f"v{part}", [P, MT, D], F32R) for part in range(2)]
        probs = room.sb("probs", [P, 2, MEM])
        t_hi = room.sb("t_hi", [P, 2, MT, BANK], F32R)
        t_lo = room.sb("t_lo", [P, 2, MT, BANK], F32R)
        o_p = room.sb("o_p", [P, 2, 2 * BANK])
        o_hi = o_p[:, :, 0:BANK].bitcast(F32R)
        o_lo = o_p[:, :, BANK:2 * BANK].bitcast(F32R)
        weight = Resident(room, "w", w_cq, stage=o_p)
        top = room.sb("top", [P, 4])
        minus = room.sb("minus", [P, 4])
        total = room.sb("total", [P, 4])
        share = room.sb("share", [P, 4])
        sum_s = [room.bank(f"sum_s{j}") for j in range(2)]
        turned = room.bank("turned_p")
        sum_q = room.bank("sum_q")
        sum_o = [room.bank(f"sum_o{j}") for j in range(2)]
        s_ident = room.sem("s_ident")
        s_kv = room.sem("s_kv")
        s_s = room.sem("s_scores")
        s_max = room.sem("s_max")
        s_minus = room.sem("s_minus")
        s_exp = room.sem("s_exp")
        s_share = room.sem("s_share")
        s_p = room.sem("s_probs")
        s_t = room.sem("s_turned_p")
        s_thi = room.sem("s_turned_p_hi")
        s_tlo = room.sem("s_turned_p_lo")
        s_q = room.sem("s_q")
        s_qhi = room.sem("s_q_hi")
        s_qlo = room.sem("s_q_lo")
        s_o = room.sem("s_o")
        s_ohi = room.sem("s_o_hi")
        s_olo = room.sem("s_o_lo")
        s_st = [room.sem(f"s_st{j}") for j in range(2)]

        def events(more):
            order = []
            for u in range(UNITS):
                h, t = divmod(u, BT)
                order.append(("S", u))
                if more:
                    order += [("f", u)] * (u < BT) + [("g", u - 1)] * (1 <= u < BT + 1) \
                        + [("F", u - 2)] * (2 <= u < BT + 2) + [("Q", u - 6)] * (u >= 6)
                if u >= 2:
                    order.append(("T", u - 2))
                if h >= 1 and t == 2:
                    order.append(("O", h - 1))
            tail = [("T", UNITS - 2), ("Q", 10), ("T", UNITS - 1), ("Q", 11), ("Q", 12), ("O", XH - 1),
                    ("Q", 13), ("Q", 14), ("Q", 15)]
            return order + [e for e in tail if more or e[0] != "Q"]

        first = [(kind, t) for t in range(BT) for kind in "fgF"] + [("Q", x) for x in range(2 * KT)]

        def run(engine, do):
            for kind, x in first:
                if kind in do:
                    do[kind](-1, x)
            with engine.Fori(0, NBLK - 1) as b:
                for kind, x in events(True):
                    if kind in do:
                        do[kind](b, x)
            for kind, x in events(False):
                if kind in do:
                    do[kind](NBLK - 1, x)

        with nc.Block() as block:
            @block.sync
            def _(sp):
                sp.dma_start(norm.gain[:, :], g_cross.to_broadcast([P, D])).then_inc(norm.s_gain, 16)
                weight.load(sp)
                for part in range(2):
                    sp.dma_start(raw(k_p[part][:, :, :].rearrange("p k t -> p (k t)")), kx_d[part]).then_inc(s_kv, 16)
                    sp.dma_start(raw(v_p[part][:, :, :].rearrange("p k t -> p (k t)")), vx_d[part]).then_inc(s_kv, 16)

                def load(b, t):
                    n = b * BT + BT + t
                    sp.wait_ge(norm.s_xn, free(n))
                    sp.dma_start(norm.x[:, t % 2, :], rows_of(x2_d, n)).then_inc(norm.s_x[t % 2], 16)

                def store(b, h):
                    for d in range(DT):
                        c = b * KT + h * DT + d
                        sp.wait_ge(s_olo, made(c))
                        tok = slice(b * BANK, (b + 1) * BANK) if isinstance(b, int) else bass.ds(b * BANK, BANK)
                        sp.dma_start(o_d[0, h * DT + d, :, tok], raw(o_hi[:, d, :])).then_inc(s_st[d], 16)
                        sp.dma_start(o_d[1, h * DT + d, :, tok], raw(o_lo[:, d, :])).then_inc(s_st[d], 16)

                run(sp, {"f": load, "O": store})
                for d in range(DT):
                    sp.wait_ge(s_st[d], 32 * NBLK * XH + 32)

            @block.gpsimd
            def _(pool):
                make_identity(room, pool, ident, s_ident)
                norm.start_pool(pool)

                def square_root(b, t):
                    norm.pool_rsqrt(pool, b * BT + BT + t, t % 2)

                run(pool, {"f": square_root})

            @block.scalar
            def _(act):
                norm.start_act(act)
                act.sem_inc(s_exp, RING)
                for d in range(DT):
                    act.sem_inc(s_st[d], 32)
                weight.high(act)

                def square(b, t):
                    norm.act_square(act, b * BT + BT + t, t % 2, b * (BT // 2) + BT // 2 + t // 2)

                def block_high(b, t):
                    for c in range(2):
                        norm.act_hi(act, b * BT + BT + t, c, h_hi[:, 4 * c:4 * c + 4, t * P:(t + 1) * P])

                def exps(b, u):
                    n = b * UNITS + u
                    act.wait_ge(s_minus, n + 1)
                    act.wait_ge(s_t, n - 1 + RING)
                    act.activation(probs[:, u % 2, :], sum_s[u % 2][:, 0:MEM], ACT.Exp, bias=minus[:, u % 4:u % 4 + 1],
                                   scale=XD ** -0.5, accum_out=total[:, u % 4:u % 4 + 1]).then_inc(s_exp, 1)

                def probs_high(b, u):
                    h, t = divmod(u, BT)
                    act.wait_ge(s_o, b * KT + h * DT - DT + 4)
                    act.wait_ge(s_t, b * UNITS + u + 1 + RING)
                    act.activation(t_hi[:, h % 2, :, t * P:(t + 1) * P],
                                   turned[:, 0:MEM].rearrange("p (k t) -> p k t", k=MT), ACT.Copy).then_inc(s_thi, 1)

                def queries_high(b, x):
                    if x % 2 == 1:
                        m = x // 2
                        act.wait_ge(s_q, b * KT + KT + m + 1)
                        act.activation(q_hi[:, m, :], sum_q[:, :], ACT.Copy).then_inc(s_qhi, 1)

                def out_high(b, h):
                    for d in range(DT):
                        act.wait_ge(s_st[d], b * (32 * XH) + 32 * h + 32)
                        act.wait_ge(s_o, b * KT + h * DT + d + 1 + 4)
                        act.activation(o_hi[:, d, :], sum_o[d][:, :], ACT.Copy).then_inc(s_ohi, 1)

                run(act, {"f": square, "F": block_high, "S": exps, "T": probs_high, "Q": queries_high,
                          "O": out_high})

            @block.vector
            def _(dve):
                norm.start_dve(dve)
                dve.sem_inc(s_olo, RING)
                dve.sem_inc(s_qlo, 1)
                dve.sem_inc(s_tlo, 1)
                weight.low(dve)

                def scale(b, t):
                    norm.dve_scale(dve, b * BT + BT + t, t % 2)

                def block_low(b, t):
                    tok = slice(t * P, (t + 1) * P)
                    for c in range(2):
                        norm.dve_lo(dve, b * BT + BT + t, c, h_lo[:, 4 * c:4 * c + 4, tok],
                                    h_hi[:, 4 * c:4 * c + 4, tok])

                def maxima(b, u):
                    n = b * UNITS + u
                    dve.wait_ge(s_s, n + 1)
                    dve.reduce_max(top[:, u % 4:u % 4 + 1], sum_s[u % 2][:, 0:MEM], axis=AX.X).then_inc(s_max, 1)
                    dve.wait_ge(s_max, n + 1)
                    dve.tensor_scalar(minus[:, u % 4:u % 4 + 1], top[:, u % 4:u % 4 + 1], -(XD ** -0.5), None,
                                      ALU.mult).then_inc(s_minus, 1)
                    if u >= 1:
                        divide(b, u - 1)

                def divide(b, u):
                    n = b * UNITS + u
                    dve.wait_ge(s_exp, n + 1 + RING)
                    dve.reciprocal(share[:, u % 4:u % 4 + 1], total[:, u % 4:u % 4 + 1]).then_inc(s_share, 1)
                    dve.wait_ge(s_share, n + 1)
                    dve.tensor_scalar(probs[:, u % 2, :], probs[:, u % 2, :], share[:, u % 4:u % 4 + 1], None,
                                      ALU.mult).then_inc(s_p, 1)

                def probs_low(b, u):
                    h, t = divmod(u, BT)
                    if u == UNITS - 2:
                        divide(b, UNITS - 1)
                    dve.wait_ge(s_thi, b * UNITS + u + 1)
                    tok = slice(t * P, (t + 1) * P)
                    dve.tensor_tensor(t_lo[:, h % 2, :, tok], turned[:, 0:MEM].rearrange("p (k t) -> p k t", k=MT),
                                      raw(t_hi[:, h % 2, :, tok]), ALU.subtract).then_inc(s_tlo, 1)

                def queries_low(b, x):
                    if x % 2 == 1:
                        m = x // 2
                        dve.wait_ge(s_qhi, b * KT + KT + m + 1)
                        dve.tensor_tensor(q_lo[:, m, :], sum_q[:, :], raw(q_hi[:, m, :]),
                                          ALU.subtract).then_inc(s_qlo, 1)

                def out_low(b, h):
                    for d in range(DT):
                        dve.wait_ge(s_ohi, b * KT + h * DT + d + 1)
                        dve.tensor_tensor(o_lo[:, d, :], sum_o[d][:, :], raw(o_hi[:, d, :]),
                                          ALU.subtract).then_inc(s_olo, 1)

                run(dve, {"g": scale, "F": block_low, "S": maxima, "T": probs_low, "Q": queries_low,
                          "O": out_low})

            @block.tensor
            def _(pe):
                norm.start_pe(pe)
                pe.sem_inc(s_t, RING)
                pe.sem_inc(s_o, 4)
                pe.wait_ge(s_ident, 2)
                pe.wait_ge(weight.s_lo, KT)
                pe.wait_ge(s_kv, 64)

                def turn_block(b, t):
                    norm.pe_turn(pe, ident[:, :], b * BT + BT + t, t % 2)

                def queries(b, x):
                    m, part = divmod(x, 2)
                    if x == 0:
                        pe.wait_ge(norm.s_lo, (b * BT + BT + BT) * 2 + RING)
                    if part == 0:
                        pe.wait_ge(s_qlo, b * KT + KT + m + 1)
                    for k in range(part * KT // 2, (part + 1) * KT // 2):
                        last = split3(pe, sum_q[:, :], weight.hi[:, k, m * P:(m + 1) * P],
                                      weight.lo[:, k, m * P:(m + 1) * P], h_hi[:, k, :], h_lo[:, k, :],
                                      k == 0, k == KT - 1)
                    if part == 1:
                        last.then_inc(s_q, 1)

                def score(b, u):
                    h, t = divmod(u, BT)
                    n = b * UNITS + u
                    if u % BT == 0:
                        pe.wait_ge(s_qlo, b * KT + (h + 1) * DT + 1)
                    pe.wait_ge(s_exp, n - 1 + RING)
                    for d in range(DT):
                        m = h * DT + d
                        tok = slice(t * P, (t + 1) * P)
                        last = split3(pe, sum_s[u % 2][:, 0:MEM], q_hi[:, m, tok], q_lo[:, m, tok],
                                      k_p[0][:, m, :], k_p[1][:, m, :], d == 0, d == DT - 1)
                    last.then_inc(s_s, 1)

                def turn(b, u):
                    n = b * UNITS + u
                    pe.wait_ge(s_p, n + 1)
                    pe.wait_ge(s_tlo, n + 1)
                    for k in range(MT):
                        last = pe.transpose(turned[:, k * P:(k + 1) * P], probs[:, u % 2, k * P:(k + 1) * P],
                                            ident[:, :])
                    last.then_inc(s_t, 1)

                def values(b, h):
                    pe.wait_ge(s_tlo, b * UNITS + (h + 1) * BT + 1)
                    for d in range(DT):
                        c = b * KT + h * DT + d
                        pe.wait_ge(s_olo, c + 1 - DT + RING)
                        dims = slice((h * DT + d) * P, (h * DT + d + 1) * P)
                        for k in range(MT):
                            last = split3(pe, sum_o[d][:, :], v_p[0][:, k, dims], v_p[1][:, k, dims],
                                          t_hi[:, h % 2, k, :], t_lo[:, h % 2, k, :], k == 0, k == MT - 1)
                        last.then_inc(s_o, 1)

                run(pe, {"F": turn_block, "Q": queries, "S": score, "T": turn, "O": values})


def stage_cross_out(nc, o_d, w_co, x2_d, g_ffn, x3_d, h_d):
    with ExitStack() as ctx:
        room = Room(nc, ctx, "xout")
        out = room.sb("out", [P, 2, D])
        norm = Norm(room, x=out)
        weight = Resident(room, "w", w_co)
        ident = room.sb("ident", [P, P])
        o_p = [room.sb(f"o{part}", [P, 2, KT, P], F32R) for part in range(2)]
        res = room.sb("res", [P, 2, D])
        h = room.sb("h", [P, 2, KT, P])
        acc = [room.bank(f"acc{i}") for i in range(4)]
        s_ident = room.sem("s_ident")
        s_o = [room.sem(f"s_o{j}") for j in range(2)]
        s_acc = room.sem("s_acc")
        s_sum = room.sem("s_sum")
        s_stx = [room.sem(f"s_stx{j}") for j in range(2)]
        s_sth = [room.sem(f"s_sth{j}") for j in range(2)]
        PAIRS = NT // 2

        with nc.Block() as block:
            @block.sync
            def _(sp):
                def load(n, j):
                    for part in range(2):
                        tok = slice(n * P, (n + 1) * P) if isinstance(n, int) else bass.ds(n * P, P)
                        sp.dma_start(raw(o_p[part][:, j, :, :]),
                                     o_d[part, :, :, tok].rearrange("k p t -> p k t")).then_inc(s_o[j], 16)
                    sp.dma_start(res[:, j, :], rows_of(x2_d, n)).then_inc(s_o[j], 16)

                sp.dma_start(norm.gain[:, :], g_ffn.to_broadcast([P, D])).then_inc(norm.s_gain, 16)
                for j in range(2):
                    load(j, j)
                weight.load(sp)

                def pair(i, more):
                    for j in range(2):
                        n = i * 2 + j
                        tok = slice(n * P, (n + 1) * P) if isinstance(n, int) else bass.ds(n * P, P)
                        sp.wait_ge(s_sum, n * 2 + 2 + 4)
                        sp.dma_start(rows_of(x3_d, n), out[:, j, :]).then_inc(s_stx[j], 16)
                        if more:
                            load(n + 2, j)
                        sp.wait_ge(norm.s_lo, n * 2 + 2 + RING)
                        room.gate(sp)
                        sp.dma_start(h_d[:, :, tok].rearrange("k p t -> p k t"),
                                     h[:, j, :, :]).then_inc(s_sth[j], 16)

                over_pairs(sp, PAIRS, pair)
                for j in range(2):
                    sp.wait_ge(s_stx[j], 16 * PAIRS + 16)
                    sp.wait_ge(s_sth[j], 16 * PAIRS + 16)

            @block.gpsimd
            def _(pool):
                make_identity(room, pool, ident, s_ident)
                norm.start_pool(pool)
                with pool.Fori(0, PAIRS) as i:
                    for j in range(2):
                        norm.pool_rsqrt(pool, i * 2 + j, j)

            @block.scalar
            def _(act):
                norm.start_act(act)
                for j in range(2):
                    act.sem_inc(s_sth[j], 16)
                weight.high(act)
                with act.Fori(0, PAIRS) as i:
                    for j in range(2):
                        n = i * 2 + j
                        act.wait_ge(s_sum, n * 2 + 2 + 4)
                        norm.act_square(act, n, j, None)
                        act.wait_ge(s_sth[j], 16 * i + 16)
                        for b in range(2):
                            norm.act_whole(act, n, b, h[:, j, 4 * b:4 * b + 4, :])

            @block.vector
            def _(dve):
                norm.start_dve(dve)
                dve.sem_inc(s_sum, 4)
                for j in range(2):
                    dve.sem_inc(s_stx[j], 16)
                weight.low(dve)

                def total(i, j):
                    n = i * 2 + j
                    dve.wait_ge(s_o[j], i * 48 + 48)
                    dve.wait_ge(s_stx[j], 16 * i + 16)
                    for b in range(2):
                        cols = slice(b * BANK, (b + 1) * BANK)
                        dve.wait_ge(s_acc, n * 2 + b + 1 + 4)
                        dve.tensor_tensor(out[:, j, cols], acc[j * 2 + b][:, :], res[:, j, cols],
                                          ALU.add).then_inc(s_sum, 1)

                def shape(n, j):
                    norm.dve_scale(dve, n, j)

                with dve.Fori(0, PAIRS) as i:
                    for j in range(2):
                        total(i, j)
                        shape(i * 2 + j, j)

            @block.tensor
            def _(pe):
                norm.start_pe(pe)
                pe.sem_inc(s_acc, 4)
                pe.wait_ge(s_ident, 2)
                pe.wait_ge(weight.s_lo, KT)

                def multiply(i, j, between):
                    n = i * 2 + j
                    pe.wait_ge(s_o[j], i * 48 + 48)
                    for b in range(2):
                        cols = slice(b * BANK, (b + 1) * BANK)
                        pe.wait_ge(s_sum, n * 2 + b + 1)
                        for k in range(KT):
                            last = split3(pe, acc[j * 2 + b][:, :], o_p[0][:, j, k, :], o_p[1][:, j, k, :],
                                          weight.hi[:, k, cols], weight.lo[:, k, cols], k == 0, k == KT - 1)
                        last.then_inc(s_acc, 1)
                        if b == 0:
                            between()

                def turn(n, j):
                    norm.pe_turn(pe, ident[:, :], n, j)

                multiply(0, 0, lambda: None)
                multiply(0, 1, lambda: turn(0, 0))
                with pe.Fori(1, PAIRS) as i:
                    multiply(i, 0, lambda: turn(i * 2 - 1, 1))
                    multiply(i, 1, lambda: turn(i * 2, 0))
                turn(NT - 1, 1)


def stage_ffn(nc, h_d, x3_d, w_gate, w_up, w_down, g_final, out_d):
    with ExitStack() as ctx:
        room = Room(nc, ctx, "ffn")
        BLK = HALF // BANK
        DN = HT * 2
        h_p = [room.sb(f"h{part}", [P, KT, HALF], F32R) for part in range(2)]
        h_raw = room.sb("h_raw", [P, 2, HALF])
        y = room.sb("y", [P, HT, D])
        kinds = ("gate", "up", "down")
        w_raw = {c: room.sb(f"{c}_raw", [P, D]) for c in kinds}
        w_hi = {c: room.sb(f"{c}_hi", [P, 2, D], F32R) for c in kinds}
        w_lo = {c: room.sb(f"{c}_lo", [P, 2, D], F32R) for c in kinds}
        silu = room.sb("silu", [P, BLK, BANK])
        a = room.sb("a", [P, BLK, BANK])
        a_hi = room.sb("a_hi", [P, 2, HALF], F32R)
        a_lo = room.sb("a_lo", [P, 2, HALF], F32R)
        gain = room.sb("gain", [P, D])
        ss = room.sb("ss", [P, HT])
        ms = room.sb("ms", [P, HT])
        rs = room.sb("rs", [P, HT])
        power = room.sb("power", [P, HT])
        sum_g = [room.bank(f"sum_g{b}") for b in range(BLK)]
        sum_u = [room.bank(f"sum_u{b}") for b in range(BLK)]
        sum_d = [room.bank(f"sum_d{b}") for b in range(4)]
        s_h = [room.sem(f"s_h{j}") for j in range(2)]
        s_hhi = room.sem("s_h_hi")
        s_hlo = room.sem("s_h_lo")
        s_y = room.sem("s_y")
        s_gain = room.sem("s_gain")
        s_w = {c: room.sem(f"s_{c}_in") for c in kinds}
        s_whi = {c: room.sem(f"s_{c}_hi") for c in kinds}
        s_wlo = {c: room.sem(f"s_{c}_lo") for c in kinds}
        s_g = room.sem("s_gate_sum")
        s_u = room.sem("s_up_sum")
        s_dn = room.sem("s_down_sum")
        s_silu = room.sem("s_silu")
        s_a = room.sem("s_a")
        s_ahi = room.sem("s_a_hi")
        s_alo = room.sem("s_a_lo")
        s_add = room.sem("s_added")
        s_ss = room.sem("s_ss")
        s_rs = room.sem("s_rs")
        s_fin = room.sem("s_fin")
        s_st = [room.sem(f"s_st{j}") for j in range(2)]
        source = {"gate": w_gate, "up": w_up, "down": w_down}

        with nc.Block() as block:
            @block.sync
            def _(sp):
                def load(c, F, f):
                    sp.wait_ge(s_wlo[c], F + 1)
                    w = source[c][f] if isinstance(f, int) else \
                        source[c][bass.ds(f, 1), :, :].rearrange("a p c -> p (a c)")
                    sp.dma_start(w_raw[c][:, :], w).then_inc(s_w[c], 16)

                sp.dma_start(gain[:, :], g_final.to_broadcast([P, D])).then_inc(s_gain, 16)
                def rows(hf, t):
                    return slice(hf * HALF + t * P, hf * HALF + (t + 1) * P)

                def load_y(hf, t):
                    sp.dma_start(y[:, t, :], x3_d[rows(hf, t), :]).then_inc(s_y, 16)

                def stored(hf, t):
                    sp.wait_ge(s_st[t % 2], 16 * (hf * HT // 2 + t // 2 + 1))

                def finish(hf, then):
                    for t in range(HT):
                        sp.wait_ge(s_fin, hf * HT + t + 1)
                        sp.dma_start(out_d[rows(hf, t), :], y[:, t, :]).then_inc(s_st[t % 2], 16)
                        if t >= 1:
                            stored(hf, t - 1)
                            then(t - 1)
                    stored(hf, HT - 1)
                    then(HT - 1)

                for hf in range(2):
                    for k in range(KT):
                        sp.wait_ge(s_hlo, hf * KT + k + 1)
                        sp.dma_start(h_raw[:, k % 2, :], h_d[k, :, hf * HALF:(hf + 1) * HALF]).then_inc(s_h[k % 2], 16)
                        if k == 1:
                            for c in kinds:
                                load(c, hf * FT, 0)
                    for c in kinds:
                        load(c, hf * FT + 1, 1)
                    if hf == 0:
                        for t in range(HT):
                            load_y(0, t)
                    else:
                        finish(0, lambda t: load_y(1, t))
                    with sp.Fori(2, FT) as f:
                        for c in kinds:
                            load(c, hf * FT + f, f)
                finish(1, lambda t: None)

            @block.gpsimd
            def _(pool):
                pool.memset(power[:, :], -0.5).then_inc(s_rs, 1)
                for c in kinds:
                    pool.sem_inc(s_wlo[c], 1)

                def split(F, j):
                    for c in kinds:
                        pool.wait_ge(s_w[c], F * 16 + 16)
                        if c == "down":
                            pool.wait_ge(s_dn, F * DN + DN)
                        else:
                            pool.wait_ge(s_g if c == "gate" else s_u, F * BLK + 2)
                        if not isinstance(F, int):
                            room.gate(pool)
                        pool.tensor_scalar(w_hi[c][:, j, :], w_raw[c][:, :], 1.0, 1.0,
                                           ALU.mult, ALU.mult).then_inc(s_whi[c], 1)
                        pool.wait_ge(s_whi[c], F + 1)
                        pool.tensor_tensor(w_lo[c][:, j, :], w_raw[c][:, :], raw(w_hi[c][:, j, :]),
                                           ALU.subtract).then_inc(s_wlo[c], 1)

                def factors(hf):
                    pool.wait_ge(s_ss, hf * HT + HT + 1)
                    pool.tensor_scalar(ms[:, :], ss[:, :], 1.0 / D, EPS, ALU.mult, ALU.add).then_inc(s_rs, 1)
                    pool.wait_ge(s_rs, hf * 2 + 2)
                    pool.tensor_tensor(rs[:, :], ms[:, :], power[:, :], ALU.pow).then_inc(s_rs, 1)

                for hf in range(2):
                    split(hf * FT, 0)
                    if hf == 1:
                        factors(0)
                    split(hf * FT + 1, 1)
                    with pool.Fori(1, FT // 2) as i:
                        for j in range(2):
                            split(hf * FT + i * 2 + j, j)
                factors(1)

            @block.scalar
            def _(act):
                act.sem_inc(s_silu, 2)
                act.sem_inc(s_ss, 1)

                def hidden(F, j):
                    for b in range(BLK):
                        act.wait_ge(s_g, F * BLK + b + 1 + 4)
                        act.wait_ge(s_a, F * BLK + b + 1)
                        act.activation(silu[:, b, :], sum_g[b][:, :], ACT.Silu).then_inc(s_silu, 1)
                        act.wait_ge(s_dn, F * DN + DN)
                        act.wait_ge(s_a, F * BLK + b + 1 + 2)
                        act.activation(a_hi[:, j, b * BANK:(b + 1) * BANK], a[:, b, :], ACT.Copy).then_inc(s_ahi, 1)

                def h_high(hf):
                    act.wait_ge(s_u, hf * FT * BLK + 4)
                    for k in range(KT):
                        act.wait_ge(s_h[k % 2], 16 * (hf * KT // 2 + k // 2 + 1))
                        act.activation(h_p[0][:, k, :], h_raw[:, k % 2, :], ACT.Copy).then_inc(s_hhi, 1)

                h_high(0)
                for hf in range(2):
                    with act.Fori(0, FT // 2) as i:
                        for j in range(2):
                            hidden(hf * FT + i * 2 + j, j)
                    if hf == 0:
                        h_high(1)
                    for t in range(HT):
                        act.wait_ge(s_add, hf * FT * DN + (FT - 1) * DN + 2 * t + 2 + DN)
                        act.wait_ge(s_ss, hf * HT + t + 1)
                        act.activation(silu[:, :, :].rearrange("p b c -> p (b c)"), y[:, t, :], ACT.Square,
                                       accum_out=ss[:, t:t + 1]).then_inc(s_ss, 1)
                    act.wait_ge(s_ss, hf * HT + HT + 1)

            @block.vector
            def _(dve):
                dve.sem_inc(s_a, 2)
                dve.sem_inc(s_alo, 2)
                dve.sem_inc(s_add, DN)
                dve.sem_inc(s_hlo, 2)
                dve.wait_ge(s_gain, 16)

                def product(F, b):
                    dve.wait_ge(s_silu, F * BLK + b + 1 + 2)
                    dve.wait_ge(s_alo, F * BLK + b + 1)
                    dve.wait_ge(s_u, F * BLK + b + 1 + 4)
                    dve.tensor_tensor(a[:, b, :], sum_u[b][:, :], silu[:, b, :], ALU.mult).then_inc(s_a, 1)

                def low(F, j, b):
                    dve.wait_ge(s_ahi, F * BLK + b + 1)
                    cols = slice(b * BANK, (b + 1) * BANK)
                    dve.tensor_tensor(a_lo[:, j, cols], a[:, b, :], raw(a_hi[:, j, cols]),
                                      ALU.subtract).then_inc(s_alo, 1)

                def add(F, q):
                    for z in range(DN // 4):
                        d = q * (DN // 4) + z
                        t, n = divmod(d, 2)
                        dve.wait_ge(s_dn, F * DN + d + 1 + 2 * DN)
                        dve.wait_ge(s_add, F * DN + d + 1)
                        cols = slice(n * BANK, (n + 1) * BANK)
                        dve.tensor_tensor(y[:, t, cols], sum_d[d % 4][:, :], y[:, t, cols],
                                          ALU.add).then_inc(s_add, 1)

                def both(F, j):
                    add(F - 1, 0)
                    product(F, 0)
                    add(F - 1, 1)
                    low(F, j, 0)
                    add(F - 1, 2)
                    product(F, 1)
                    add(F - 1, 3)
                    low(F, j, 1)

                def h_low(hf, k):
                    dve.wait_ge(s_hhi, hf * KT + k + 1)
                    dve.tensor_tensor(h_p[1][:, k, :], h_raw[:, k % 2, :], raw(h_p[0][:, k, :]),
                                      ALU.subtract).then_inc(s_hlo, 1)

                for k in range(KT):
                    h_low(0, k)
                for hf in range(2):
                    for b in range(BLK):
                        product(hf * FT, b)
                        low(hf * FT, 0, b)
                    dve.wait_ge(s_y, (hf + 1) * 16 * HT)
                    with dve.Fori(0, FT // 2 - 1) as i:
                        for j in range(2):
                            both(hf * FT + i * 2 + j + 1, (j + 1) % 2)
                    both(hf * FT + (FT - 1), 1)
                    for q in range(4):
                        add(hf * FT + (FT - 1), q)
                        if hf == 0:
                            h_low(1, 2 * q)
                            h_low(1, 2 * q + 1)
                    dve.wait_ge(s_rs, hf * 2 + 3)
                    for t in range(HT):
                        dve.scalar_tensor_tensor(y[:, t, :], y[:, t, :], rs[:, t:t + 1], gain[:, :],
                                                 ALU.mult, ALU.mult).then_inc(s_fin, 1)

            @block.tensor
            def _(pe):
                pe.sem_inc(s_g, 4)
                pe.sem_inc(s_u, 4)
                pe.sem_inc(s_dn, 2 * DN)

                def down(F, j, q):
                    for z in range(DN // 4):
                        d = q * (DN // 4) + z
                        t, n = divmod(d, 2)
                        pe.wait_ge(s_add, F * DN + d + 1 - 4 + DN)
                        tok, cols = slice(t * P, (t + 1) * P), slice(n * BANK, (n + 1) * BANK)
                        split3(pe, sum_d[d % 4][:, :], a_hi[:, j, tok], a_lo[:, j, tok],
                               w_hi["down"][:, j, cols], w_lo["down"][:, j, cols], True, True).then_inc(s_dn, 1)

                def make(F, j, between, tokens=None):
                    for b in range(BLK):
                        for c, bank, s_sum, s_read in (("gate", sum_g, s_g, s_silu), ("up", sum_u, s_u, s_a)):
                            pe.wait_ge(s_wlo[c], F + 2)
                            pe.wait_ge(s_read, F * BLK + b + 1)
                            cols = slice(b * BANK, (b + 1) * BANK)
                            for k in range(KT):
                                if tokens is not None and (b, c) == (0, "gate"):
                                    pe.wait_ge(s_hlo, tokens + k + 1 + 2)
                                wk = slice(k * P, (k + 1) * P)
                                last = split3(pe, bank[b][:, :], w_hi[c][:, j, wk], w_lo[c][:, j, wk],
                                              h_p[0][:, k, cols], h_p[1][:, k, cols], k == 0, k == KT - 1)
                            last.then_inc(s_sum, 1)
                            between(b * 2 + (c == "up"))

                def both(F, j):
                    def quarter(q):
                        if q == 0:
                            pe.wait_ge(s_alo, F * BLK + 2)
                            pe.wait_ge(s_wlo["down"], F + 1)
                        down(F - 1, (j + 1) % 2, q)
                    make(F, j, quarter)

                for hf in range(2):
                    make(hf * FT, 0, lambda q: None, tokens=hf * KT)
                    with pe.Fori(0, FT // 2 - 1) as i:
                        for j in range(2):
                            both(hf * FT + i * 2 + j + 1, (j + 1) % 2)
                    both(hf * FT + (FT - 1), 1)
                    pe.wait_ge(s_alo, hf * (FT * BLK) + FT * BLK + 2)
                    pe.wait_ge(s_wlo["down"], hf * FT + FT + 1)
                    for q in range(4):
                        down(hf * FT + (FT - 1), 1, q)


_INPUTS = ["x", "mem", "positions", "freq", "g_mix", "w_qk", "b_qk", "w_v", "b_v", "sinks", "rel_rev", "g_grp",
           "w_out", "g_cross", "g_mem", "w_cq", "w_xk", "w_xv", "w_co", "g_ffn", "w_gate", "w_up", "w_down",
           "g_final"]


def build(nc, a, out):
    def scratch(name, shape):
        return nc.dram_tensor(name, shape, F32, kind="Internal").ap()

    cos_d, sin_d = scratch("cos_d", [P, SEQ]), scratch("sin_d", [P, SEQ])
    ext_d = scratch("ext_d", [P, 8 * EXT])
    bias_d = scratch("bias_d", [8, P, B_WIN * P])
    kx_d, vx_d = scratch("kx_d", [2, P, KT * MEM]), scratch("vx_d", [2, P, MT * D])
    qk_d = scratch("qk_d", [2, N_QK, P, SEQ])
    v_d = scratch("v_d", [SEQ, 2 * V_GROUP])
    mix_d, x2_d, x3_d = (scratch(n, [SEQ, D]) for n in ("mix_d", "x2_d", "x3_d"))
    o_d, h_d = scratch("o_d", [2, KT, P, SEQ]), scratch("h_d", [KT, P, SEQ])

    stage_tables(nc, a["positions"], a["freq"], a["rel_rev"], cos_d, sin_d, ext_d, bias_d)
    stage_memory(nc, a["mem"], a["g_mem"], a["w_xk"], a["w_xv"], kx_d, vx_d)
    stage_qkv(nc, a["x"], a["g_mix"], a["w_qk"], a["b_qk"], a["w_v"], a["b_v"], cos_d, sin_d, qk_d, v_d)
    stage_attention(nc, "a", qk_d, v_d, mix_d, None, a["sinks"])
    stage_attention(nc, "b", qk_d, v_d, mix_d, bias_d, None)
    stage_mix(nc, mix_d, a["g_grp"], a["x"], a["w_out"], x2_d)
    stage_cross(nc, x2_d, a["g_cross"], a["w_cq"], kx_d, vx_d, o_d)
    stage_cross_out(nc, o_d, a["w_co"], x2_d, a["g_ffn"], x3_d, h_d)
    stage_ffn(nc, h_d, x3_d, a["w_gate"], a["w_up"], a["w_down"], a["g_final"], out)


def by_tile(w, width):
    rows, cols = w.shape
    w = w.reshape(rows // P, P, cols // width, width).transpose(2, 1, 0, 3)
    return w.reshape(cols // width, P, rows // P * width)


def kernel(**inputs):
    import concourse.bacc as bacc
    from concourse.bass_utils import run_bass_kernel_spmd

    a = {name: np.asarray(v) for name, v in inputs.items()}
    w_in, b_in = a["w_in"][0], a["b_in"][0]
    ends = np.cumsum([A_Q, A_KV, A_KV, B_W, B_W, B_W])
    qa, ka, va, qb, kb, vb = (slice(e - w, e) for e, w in zip(ends, (A_Q, A_KV, A_KV, B_W, B_W, B_W)))

    def joined(w):
        k = w[..., ka]
        return np.concatenate([w[..., qa], k[..., :HD], k[..., :HD], k[..., HD:], k[..., HD:],
                               w[..., qb], w[..., kb]], axis=-1)

    step = np.arange(HD // 2, dtype=np.float32) * np.float32(2.0 / HD)
    inverse = (np.float32(1.0) / (THETA ** step.astype(np.float64)).astype(np.float32)).astype(np.float32)
    freq = np.stack([np.tile(inverse, 4), np.tile(np.repeat(np.float32([-1.0, 1.0]), HD // 2), 2)], axis=1)

    arrays = {
        "x": a["x"][0], "mem": a["mem"][0], "positions": a["positions"], "freq": freq,
        "g_mix": a["g_mix"], "w_qk": by_tile(joined(w_in), P), "b_qk": joined(b_in).reshape(N_QK, P).T,
        "w_v": by_tile(np.concatenate([w_in[:, va], w_in[:, vb]], axis=1), V_GROUP),
        "b_v": np.concatenate([b_in[va], b_in[vb]])[None],
        "sinks": a["sinks"], "rel_rev": a["rel_bias"][0][:, ::-1],
        "g_grp": np.concatenate([a["g_grp_a"], a["g_grp_b"]], axis=1),
        "w_out": a["w_out"][0].reshape(KT, P, D), "g_cross": a["g_cross"], "g_mem": a["g_mem"],
        "w_cq": a["w_cq"][0].reshape(KT, P, D), "w_xk": by_tile(a["w_ckv"][0][:, :D], P),
        "w_xv": by_tile(a["w_ckv"][0][:, D:], 256), "w_co": a["w_co"][0].reshape(KT, P, D),
        "g_ffn": a["g_ffn"], "w_gate": by_tile(a["w_gate"][0], P), "w_up": by_tile(a["w_up"][0], P),
        "w_down": a["w_down"][0].reshape(FT, P, D), "g_final": a["g_final"][None],
    }
    arrays = {name: np.ascontiguousarray(arrays[name]) for name in _INPUTS}

    nc = bacc.Bacc("TRN2", target_bir_lowering=False, num_devices=1)
    aps = {n: nc.dram_tensor(f"in_{n}", v.shape, mybir.dt.from_np(v.dtype), kind="ExternalInput").ap()
           for n, v in arrays.items()}
    out = nc.dram_tensor("out", (SEQ, D), F32, kind="ExternalOutput").ap()
    build(nc, aps, out)
    r = run_bass_kernel_spmd(nc, [{f"in_{n}": v for n, v in arrays.items()}], core_ids=[0])
    return r.results[0]["out"].reshape(1, SEQ, D)
```
